# Optimizing a Trainium2 kernel written in Bass

```python
import jax, jax.numpy as jnp
from jax import lax
import numpy as np

D_MODEL = 1024
BATCH = 1
SEQ = 1024
DEPTH = 2

CHUNK = 64
N_EVEN = (DEPTH + 1) // 2
N_ODD = DEPTH // 2
D_FF = 4 * D_MODEL
RMS_EPS = 1e-6
RET_WIDTH = D_MODEL // 2
RET_HEADS = 4
RET_HEAD_DIM = RET_WIDTH // RET_HEADS
RET_ROPE_BASE = 10000.0
GN_EPS = 1e-5
POOL_WIDTH = D_MODEL - RET_WIDTH
POOL_WINDOWS = (2, 4, 8, 16)
POOL_GROUPS = len(POOL_WINDOWS)
POOL_GROUP_DIM = POOL_WIDTH // POOL_GROUPS
AB_IN_WIDTH = 4 * RET_WIDTH + POOL_WIDTH
AB_OUT_WIDTH = RET_WIDTH + POOL_WIDTH
ATT_HEADS = 16
ATT_HEAD_DIM = D_MODEL // ATT_HEADS
LEFT_CHUNKS = 8
BAND = (LEFT_CHUNKS + 1) * CHUNK
REL_CLIP = 128
N_REL = 2 * REL_CLIP + 1
NEG_INF = -1e30

kernel_name = "hybrid_retention_pool_chunkattn_trunk"

def rms_norm(x, g):
    xf = x.astype(jnp.float32)
    y = xf * lax.rsqrt(jnp.mean(xf * xf, axis=-1, keepdims=True) + RMS_EPS)
    return (y * g.astype(jnp.float32)).astype(x.dtype)

def rotary(x):
    S, d = x.shape[1], x.shape[-1]
    inv_freq = 1.0 / (RET_ROPE_BASE ** jnp.linspace(0.0, 1.0, d // 2, dtype=jnp.float32))
    ang = jnp.arange(S, dtype=jnp.float32)[:, None] * inv_freq[None, :]
    cos = jnp.cos(ang)[None, :, None, :]
    sin = jnp.sin(ang)[None, :, None, :]
    x1, x2 = x[..., 0::2], x[..., 1::2]
    return jnp.stack([x1 * cos - x2 * sin, x1 * sin + x2 * cos], axis=-1).reshape(x.shape)

def retention(q, k, v):
    B, S, H, d = q.shape
    nc = S // CHUNK
    log_g = jnp.log1p(-jnp.power(2.0, -5.0 - jnp.arange(H, dtype=jnp.float32)))
    pos = jnp.arange(CHUNK, dtype=jnp.float32)
    intra_decay = jnp.exp(jnp.abs(pos[:, None] - pos[None, :])[None] * log_g[:, None, None])
    q_decay = jnp.exp((pos[:, None] + 1.0) * log_g[None, :])
    k_decay = jnp.exp((CHUNK - 1.0 - pos[:, None]) * log_g[None, :])
    chunk_decay = jnp.exp(CHUNK * log_g)

    qc = q.reshape(B, nc, CHUNK, H, d)
    kc = k.reshape(B, nc, CHUNK, H, d)
    vc = v.reshape(B, nc, CHUNK, H, d)
    scores = jnp.einsum('bcnhd,bcmhd->bchnm', qc, kc) * intra_decay
    intra = jnp.einsum('bchnm,bcmhe->bcnhe', scores, vc)

    def step(state, inp):
        q_i, k_i, v_i = inp
        cross = jnp.einsum('bnhd,bhde->bnhe', q_i * q_decay[:, :, None], state)
        state = state * chunk_decay[:, None, None] + jnp.einsum(
            'bmhd,bmhe->bhde', k_i * k_decay[:, :, None], v_i)
        return state, cross

    xs = (jnp.moveaxis(qc, 1, 0), jnp.moveaxis(kc, 1, 0), jnp.moveaxis(vc, 1, 0))
    state0 = jnp.zeros((B, H, d, d), jnp.float32)
    _, cross = lax.scan(step, state0, xs)
    out = intra + jnp.moveaxis(cross, 0, 1)
    return out.reshape(B, S, H, d)

def head_group_norm(o, g):
    B, S, H, d = o.shape
    mu = jnp.mean(o, axis=-1, keepdims=True)
    var = jnp.mean(jnp.square(o - mu), axis=-1, keepdims=True)
    y = (o - mu) * lax.rsqrt(var + GN_EPS)
    return y.reshape(B, S, H * d) * g

def multiscale_pool(p, w_group, scale):
    B, S, _ = p.shape
    pf = p.astype(jnp.float32).reshape(B, S, POOL_GROUPS, POOL_GROUP_DIM)
    csum = lax.cumsum(pf, axis=1)
    t = jnp.arange(S)
    outs = []
    for gi, w in enumerate(POOL_WINDOWS):
        c = csum[:, :, gi]
        lagged = jnp.pad(c, ((0, 0), (w, 0), (0, 0)))[:, :S]
        count = jnp.minimum(t + 1, w).astype(jnp.float32)[None, :, None]
        outs.append((c - lagged) / count - pf[:, :, gi])
    pooled = jnp.stack(outs, axis=2)
    mixed = jnp.einsum('bsgc,gce->bsge', pooled, w_group.astype(jnp.float32))
    return (mixed.reshape(B, S, POOL_WIDTH) * scale.astype(jnp.float32)).astype(p.dtype)

def retention_pool_mixer(h, w_in, gn_gain, w_pool, pool_scale, w_out):
    B, S, _ = h.shape
    z = h @ w_in
    q, k, v, g, p = jnp.split(
        z, [RET_WIDTH, 2 * RET_WIDTH, 3 * RET_WIDTH, 4 * RET_WIDTH], axis=-1)

    def heads(t):
        return t.astype(jnp.float32).reshape(B, S, RET_HEADS, RET_HEAD_DIM)

    qh = rotary(heads(q))
    kh = rotary(heads(k)) * (RET_HEAD_DIM ** -0.5)
    o = retention(qh, kh, heads(v))
    o = head_group_norm(o, gn_gain.astype(jnp.float32))
    ret_out = (jax.nn.silu(g.astype(jnp.float32)) * o).astype(h.dtype)
    pool_out = multiscale_pool(p, w_pool, pool_scale)
    return jnp.concatenate([ret_out, pool_out], axis=-1) @ w_out

def chunk_attention(h, w_qkv, rel_bias, w_out):
    B, S, _ = h.shape
    nc = S // CHUNK
    q, k, v = jnp.split(h @ w_qkv, 3, axis=-1)
    q = q.reshape(B, S, ATT_HEADS, ATT_HEAD_DIM) * (ATT_HEAD_DIM ** -0.5)
    pad = ((0, 0), (LEFT_CHUNKS * CHUNK, 0), (0, 0), (0, 0))
    k = jnp.pad(k.reshape(B, S, ATT_HEADS, ATT_HEAD_DIM), pad)
    v = jnp.pad(v.reshape(B, S, ATT_HEADS, ATT_HEAD_DIM), pad)
    n_idx = jnp.arange(CHUNK)[:, None]
    j_idx = jnp.arange(BAND)[None, :]
    rel = jnp.clip(n_idx + LEFT_CHUNKS * CHUNK - j_idx, -REL_CLIP, REL_CLIP) + REL_CLIP
    bias = rel_bias.astype(jnp.float32)[:, rel]
    band_pos = jnp.arange(BAND)

    def one_chunk(c):
        q_c = lax.dynamic_slice_in_dim(q, c * CHUNK, CHUNK, axis=1)
        k_b = lax.dynamic_slice_in_dim(k, c * CHUNK, BAND, axis=1)
        v_b = lax.dynamic_slice_in_dim(v, c * CHUNK, BAND, axis=1)
        s = jnp.einsum('bnhd,bjhd->bhnj', q_c, k_b).astype(jnp.float32) + bias
        valid = band_pos >= (LEFT_CHUNKS - c) * CHUNK
        s = jnp.where(valid, s, NEG_INF)
        pr = jax.nn.softmax(s, axis=-1).astype(v_b.dtype)
        return jnp.einsum('bhnj,bjhd->bnhd', pr, v_b)

    o = lax.map(one_chunk, jnp.arange(nc))
    o = jnp.moveaxis(o, 0, 1).reshape(B, S, D_MODEL)
    return o @ w_out

def squared_relu_mlp(h, w1, w2):
    return jnp.square(jax.nn.relu(h @ w1)) @ w2

def setup_inputs(seed: int = 0) -> dict:
    key = jax.random.key(seed)
    ks = jax.random.split(key, 16)
    f32 = jnp.float32

    def nrm(k, shape, scale):
        return jax.random.normal(k, shape, f32) * scale

    return {
        "x": nrm(ks[0], (BATCH, SEQ, D_MODEL), 1.0),
        "mix_norm": 1.0 + nrm(ks[1], (DEPTH, D_MODEL), 0.05),
        "ffn_norm": 1.0 + nrm(ks[2], (DEPTH, D_MODEL), 0.05),
        "w_ffn_in": nrm(ks[3], (DEPTH, D_MODEL, D_FF), D_MODEL ** -0.5),
        "w_ffn_out": nrm(ks[4], (DEPTH, D_FF, D_MODEL), D_FF ** -0.5),
        "ab_w_in": nrm(ks[5], (N_EVEN, D_MODEL, AB_IN_WIDTH), D_MODEL ** -0.5),
        "ab_gn_gain": 1.0 + nrm(ks[6], (N_EVEN, RET_WIDTH), 0.05),
        "ab_w_pool": nrm(ks[7], (N_EVEN, POOL_GROUPS, POOL_GROUP_DIM, POOL_GROUP_DIM), POOL_GROUP_DIM ** -0.5),
        "ab_pool_scale": 1.0 + nrm(ks[8], (N_EVEN, POOL_WIDTH), 0.1),
        "ab_w_out": nrm(ks[9], (N_EVEN, AB_OUT_WIDTH, D_MODEL), AB_OUT_WIDTH ** -0.5),
        "c_w_qkv": nrm(ks[10], (N_ODD, D_MODEL, 3 * D_MODEL), D_MODEL ** -0.5),
        "c_rel_bias": nrm(ks[11], (N_ODD, ATT_HEADS, N_REL), 0.5),
        "c_w_out": nrm(ks[12], (N_ODD, D_MODEL, D_MODEL), D_MODEL ** -0.5),
        "final_norm": 1.0 + nrm(ks[13], (D_MODEL,), 0.05),
    }

def reference(x, mix_norm, ffn_norm, w_ffn_in, w_ffn_out, ab_w_in, ab_gn_gain,
              ab_w_pool, ab_pool_scale, ab_w_out, c_w_qkv, c_rel_bias, c_w_out,
              final_norm):
    for layer in range(DEPTH):
        h = rms_norm(x, mix_norm[layer])
        i = layer // 2
        if layer % 2 == 0:
            x = x + retention_pool_mixer(h, ab_w_in[i], ab_gn_gain[i], ab_w_pool[i],
                                         ab_pool_scale[i], ab_w_out[i])
        else:
            x = x + chunk_attention(h, c_w_qkv[i], c_rel_bias[i], c_w_out[i])
        x = x + squared_relu_mlp(rms_norm(x, ffn_norm[layer]), w_ffn_in[layer], w_ffn_out[layer])
    return rms_norm(x, final_norm)


_drawn_inputs = setup_inputs


def setup_inputs(seed=0):
    import zlib

    import numpy as np

    out = dict(_drawn_inputs(seed))
    spreads = {}
    factors = {'ab_gn_gain': 2.897, 'c_rel_bias': 2.669}
    for name, (base, spread) in spreads.items():
        noise = np.random.default_rng([zlib.crc32(name.encode()), seed]).standard_normal(out[name].shape)
        drawn = base * np.exp(spread * noise) if base else spread * noise
        out[name] = __import__('jax').numpy.asarray(drawn.astype(out[name].dtype))
    for name, factor in factors.items():
        out[name] = (out[name] * factor).astype(out[name].dtype)
    return out
```

```python
from contextlib import ExitStack

import concourse.bass as bass
from concourse import mybir

P = 128
D = 1024
S = 1024
KT = D // P
HALF = 512
FB = 4
RET_HEADS = 4
POOL_WINDOWS = (2, 4, 8, 16)
POOL_GROUPS = len(POOL_WINDOWS)
EDGE = POOL_WINDOWS[-1]
ATT_GROUPS = 8
DH = 64
QT = S // P
BAND = 640
REL = 256
REL_ROW = 383
RMS_EPS = 1e-6
GN_EPS = 1e-5
MASKED = -1e30

N_OUT0 = 4 * RET_HEADS + POOL_GROUPS
N_MLP0 = N_OUT0 + KT
N_ATT = N_MLP0 + 2 * KT * FB
N_OUT1 = N_ATT + 3 * ATT_GROUPS
N_MLP1 = N_OUT1 + KT
N_UNITS = N_MLP1 + 2 * KT * FB

RET_STEPS = [(max(HALF * half, P * j), HALF * (half + 1) - max(HALF * half, P * j), j)
             for half in (0, 1) for j in range(4 * (half + 1))]
N_RET = len(RET_STEPS)

C_ID = 0
C_GAIN = C_ID + P
C_GN = C_GAIN + 5 * KT
C_PS = C_GN + RET_HEADS
C_CNT = C_PS + POOL_GROUPS
C_ALL = C_CNT + POOL_GROUPS * EDGE

F32 = mybir.dt.float32
F32R = mybir.dt.float32r
ALU = mybir.AluOpType
ACT = mybir.ActivationFunctionType


class Chain:

    def __init__(self, eng, sem):
        self.eng, self.sem, self.base, self.k = eng, sem, 0, 0

    def link(self, ins):
        ins.then_inc(self.sem, 1)
        self.k += 1
        self.eng.wait_ge(self.sem, self.base + self.k)

    def enter(self, i, per):
        outer = (self.base, self.k)
        self.base, self.k = self.base + self.k + i * per, 0
        return outer

    def leave(self, outer, per, count):
        assert self.k == per, (self.k, per)
        self.base, self.k = outer[0], outer[1] + per * count


def trunk_kernel(nc, weights, x_in, small, rot, decay, w_pool, rel, out, spill):
    with ExitStack() as ctx:
        def sb(name, shape, dt=F32):
            return ctx.enter_context(nc.sbuf_tensor(name, shape, dt))

        def sem(name):
            return ctx.enter_context(nc.semaphore(name))

        X = sb("X", [P, KT, S])
        G_hi = sb("G_hi", [P, KT, S], F32R)
        G_lo = sb("G_lo", [P, KT, S], F32R)
        A_hi = sb("A_hi", [P, KT, S], F32R)
        A_lo = sb("A_lo", [P, KT, S], F32R)
        raw = sb("raw", [P, 2, S])
        W_hi = sb("W_hi", [P, 2, KT, P], F32R)
        W_lo = sb("W_lo", [P, 2, KT, P], F32R)
        R = sb("R", [P, S])
        T = sb("T", [P, 4, S])
        C = sb("C", [P, C_ALL])
        ones_d = sb("ones_d", [P, P])
        ones_h = sb("ones_h", [P, P])
        eps = sb("eps", [P, 2])
        row = sb("row", [P, 6 * 16])

        PU = ctx.enter_context(nc.psum_tensor("PU", [P, 4, HALF], F32))
        PM = ctx.enter_context(nc.psum_tensor("PM", [P, 4, HALF], F32))
        PUf = PU[:, :, :].rearrange("p b n -> p (b n)")
        PMf = PM[:, :, :].rearrange("p b n -> p (b n)")

        qT, kT, vT, V, gate = X[:, 0, :], X[:, 1, :], X[:, 2, :], X[:, 3, :], X[:, 4, :]
        OT = X[:, 2, :]
        Xf = X[:, :, :].rearrange("p k n -> p (k n)")
        probs = [Xf[:, 5 * S + HALF * i:5 * S + HALF * (i + 1)] for i in range(3)]
        sq_head = X[:, 5, :]
        dec = X[:, 7, :]
        cosR, sinR = T[:, 0, :], T[:, 1, :]
        bias = Xf[:, 4 * S:4 * S + 2 * BAND].rearrange("p (a n) -> p a n", a=2)
        rel_t = X[:, 7, 0:2 * REL].rearrange("p (a n) -> p a n", a=2)
        O_sb = X[:, 6, :].rearrange("p (t f) -> p t f", t=QT)
        WP = X[:, 4, :]
        ident = C[:, C_ID:C_ID + P]

        raw_landed = [sem("raw_landed0"), sem("raw_landed1")]
        w_hi, w_lo = sem("w_hi"), sem("w_lo")
        unit_done = sem("unit_done")
        unit_read = sem("unit_read")
        g_src, g_hi, g_ready = sem("g_src"), sem("g_hi"), sem("g_ready")
        a_src, a_hi, a_ready = sem("a_src"), sem("a_hi"), sem("a_ready")
        sq_ready, ss_added = sem("sq_ready"), sem("ss_added")
        stat_done, sd_ready, r_ready = sem("stat_done"), sem("sd_ready"), sem("r_ready")
        x_landed = [sem(f"x_landed{m}") for m in range(KT)]
        const_landed, const_set = sem("const_landed"), sem("const_set")
        rot_landed, dec_landed, wp_landed = sem("rot_landed"), sem("dec_landed"), sem("wp_landed")
        rotated, v_turned, v_ready = sem("rotated"), sem("v_turned"), sem("v_ready")
        gate_exp = sem("gate_exp")
        score_done, p_ready, pv_done, o_evac = sem("score_done"), sem("p_ready"), sem("pv_done"), sem("o_evac")
        gn_mean, gn_centered, gn_sq, gn_var, gn_sd = (sem("gn_mean"), sem("gn_centered"), sem("gn_sq"),
                                                      sem("gn_var"), sem("gn_sd"))
        pooled, pool_mm = sem("pooled"), sem("pool_mm")
        spilled = sem("spilled")
        av_turned, av_ready = sem("av_turned"), sem("av_ready")
        b_masked, b_landed, b_ready = sem("b_masked"), sem("b_landed"), sem("b_ready")
        s_done, negm_ready, exp_done, pt_done, pt_ready, o_done, o_free, ot_done = (
            sem("s_done"), sem("negm_ready"), sem("exp_done"), sem("pt_done"), sem("pt_ready"),
            sem("o_done"), sem("o_free"), sem("ot_done"))
        y_ready, out_landed = sem("y_ready"), sem("out_landed")
        dve_step, act_step = sem("dve_step"), sem("act_step")

        block = ctx.enter_context(nc.Block())

        @block.sync
        def _(sp):
            sp.dma_start(raw[:, 0, :], weights[0]).then_inc(raw_landed[0], 16)
            sp.dma_start(raw[:, 1, :], weights[1]).then_inc(raw_landed[1], 16)
            with sp.Fori(1, N_UNITS // 2) as j:
                for s in (0, 1):
                    sp.wait_ge(w_lo, 2 * j + (s - 1))
                    sp.dma_start(raw[:, s:s + 1, :],
                                 weights[bass.ds(2 * j + s, 1)].rearrange("u p n -> p u n")).then_inc(raw_landed[s], 16)

        @block.gpsimd
        def _(pool):
            pool.dma_start(C[:, :], small).then_inc(const_landed, 16)
            for m in range(KT):
                pool.dma_start(X[:, m, :], x_in[m]).then_inc(x_landed[m], 16)
            pool.wait_ge(r_ready, 1)
            pool.dma_start(T[:, 0:2, :], rot).then_inc(rot_landed, 16)
            pool.dma_start(dec, decay[0]).then_inc(dec_landed, 16)
            with pool.Fori(1, RET_HEADS) as h:
                pool.wait_ge(p_ready, h * N_RET)
                pool.dma_start(X[:, 7:8, :], decay[bass.ds(h, 1)].rearrange("h p n -> p h n")).then_inc(dec_landed, 16)
            pool.wait_ge(a_src, RET_HEADS)
            pool.dma_start(WP[:, 0:POOL_GROUPS * P], w_pool).then_inc(wp_landed, 16)
            pool.wait_ge(a_ready, KT)
            for m in range(KT):
                pool.dma_start(X[:, m, :], x_in[m]).then_inc(x_landed[m], 16)
            for m in range(KT):
                pool.wait_ge(unit_read, N_ATT - KT + m + 1)
                pool.dma_start(spill[m], X[:, m, :]).then_inc(spilled, 16)
            pool.wait_ge(spilled, 16 * KT)
            pool.wait_ge(r_ready, 3)
            for a in (0, 1):
                pool.memset(bias[0:DH, a, BAND - DH:BAND], MASKED).then_inc(b_masked, 1)
                pool.memset(bias[DH:P, a, 0:DH], MASKED).then_inc(b_masked, 1)

            def bias_tiles(g):
                pool.dma_start(rel_t, bass.AP(tensor=rel.tensor, offset=g * (2 * REL_ROW),
                                              ap=[[1, P], [REL_ROW, 2], [1, REL]])).then_inc(b_landed, 16)
                pool.wait_ge(b_landed, g * 16 + 16)
                for a in (0, 1):
                    for rows, first, end in ((slice(0, DH), 0, BAND - DH), (slice(DH, P), DH, BAND)):
                        near = rel_t[rows, a, REL - (end - (BAND - REL)):REL][:, ::-1]
                        far = rel_t[rows, a, REL - 1:REL].to_broadcast([DH, BAND - REL - first])
                        zero = row[rows, 94:95]
                        for to, of in ((slice(BAND - REL, end), near), (slice(first, BAND - REL), far)):
                            pool.tensor_tensor(bias[rows, a, to], of, zero.to_broadcast([DH, to.stop - to.start]),
                                               ALU.add).then_inc(b_ready, 1)

            bias_tiles(0)
            with pool.Fori(1, ATT_GROUPS) as g:
                pool.wait_ge(negm_ready, g * (2 * QT))
                bias_tiles(g)
            pool.wait_ge(a_ready, KT * (FB + 2))
            for m in range(KT):
                pool.dma_start(X[:, m, :], spill[m]).then_inc(x_landed[m], 16)
            for m in range(KT):
                pool.wait_ge(y_ready, m + 1)
                pool.dma_start(out[m], X[:, m, :]).then_inc(out_landed, 16)
            pool.wait_ge(out_landed, 16 * KT)

        @block.tensor
        def _(pe):
            def unit(j, s, hi, lo, ready=None, base=0):
                pe.wait_ge(w_lo, 2 * j + s + 1)
                if not (isinstance(j, int) and j == 0):
                    pe.wait_ge(unit_read, 2 * j + s - 1)
                for k in range(KT):
                    if ready is not None:
                        pe.wait_ge(ready, base + k + 1)
                    for n, (w, x) in enumerate(((W_hi, hi), (W_hi, lo), (W_lo, hi))):
                        for half in (0, 1):
                            last = pe.matmul(PU[:, 2 * s + half, :], w[:, s, k, :],
                                             x[:, k, HALF * half:HALF * (half + 1)],
                                             start=(k == 0 and n == 0), stop=(k == KT - 1 and n == 2))
                last.then_inc(unit_done, 1)

            def phase(j0, hi, lo, ready, base, pairs=KT // 2):
                unit(j0, 0, hi, lo, ready, base)
                unit(j0, 1, hi, lo)
                with pe.Fori(1, pairs) as i:
                    for s in (0, 1):
                        unit(j0 + i, s, hi, lo)

            def mean_of_squares(v):
                pe.wait_ge(ss_added, KT * (v + 1))
                for half in (0, 1):
                    last = pe.matmul(PM[:, half, :], ones_d[:, :], R[:, HALF * half:HALF * (half + 1)],
                                     start=True, stop=True)
                last.then_inc(stat_done, 1)

            def group_mean(h):
                pe.wait_ge(o_evac, 2 * h + 2)
                for half in (0, 1):
                    last = pe.matmul(PM[:, half, :], ones_h[:, :], OT[:, HALF * half:HALF * (half + 1)],
                                     start=True, stop=True)
                last.then_inc(gn_mean, 1)

            def group_var(h):
                pe.wait_ge(gn_sq, h + 1)
                for half in (0, 1):
                    last = pe.matmul(PM[:, 2 + half, :], ones_h[:, :], sq_head[:, HALF * half:HALF * (half + 1)],
                                     start=True, stop=True)
                last.then_inc(gn_var, 1)

            def retention(h, first):
                pe.wait_ge(unit_read, 4 * h + 3)
                for c in range(QT):
                    last = pe.transpose(PMf[:, P * c:P * (c + 1)], vT[:, P * c:P * (c + 1)], ident)
                last.then_inc(v_turned, 1)
                pe.wait_ge(v_ready, h + 1)
                pe.wait_ge(rotated, 2 * h + 2)
                if not first:
                    pe.wait_ge(gn_sd, h)
                for x in range(N_RET + 3):
                    if x >= 3:
                        y = x - 3
                        q0, n, kt = RET_STEPS[y]
                        pe.wait_ge(p_ready, h * N_RET + (y + 1))
                        if kt == 0 and q0:
                            pe.wait_ge(o_evac, 2 * h + 1)
                        end = kt == (3 if q0 < HALF else 7)
                        pe.matmul(PM[:, 3, q0 % HALF:q0 % HALF + n], V[:, P * kt:P * (kt + 1)], probs[y % 3][:, 0:n],
                                  start=(kt == 0), stop=end).then_inc(pv_done, 1)
                    if x < N_RET:
                        q0, n, kt = RET_STEPS[x]
                        pe.matmul(PM[:, x % 3, 0:n], kT[:, P * kt:P * (kt + 1)], qT[:, q0:q0 + n],
                                  start=True, stop=True).then_inc(score_done, 1)

            def pool_product(i):
                if i == 0:
                    pe.wait_ge(wp_landed, 16)
                pe.wait_ge(pooled, i + 1)
                if i == 1:
                    pe.wait_ge(gn_sd, RET_HEADS)
                if i >= 2:
                    pe.wait_ge(a_src, RET_HEADS + i - 1)
                for half in (0, 1):
                    last = pe.matmul(PM[:, 2 * (i % 2) + half, :], WP[:, P * i:P * (i + 1)],
                                     X[:, 6 + i % 2, HALF * half:HALF * (half + 1)], start=True, stop=True)
                last.then_inc(pool_mm, 1)

            pe.wait_ge(const_landed, 16)
            pe.wait_ge(const_set, 1)
            for s in (0, 1):
                unit(0, s, G_hi, G_lo, g_ready if s == 0 else None)
                if s == 0:
                    mean_of_squares(0)
            for s in (0, 1):
                unit(1, s, G_hi, G_lo)
            retention(0, True)
            with pe.Fori(1, RET_HEADS) as h:
                unit(2 * h, 0, G_hi, G_lo)
                group_mean(h - 1)
                unit(2 * h, 1, G_hi, G_lo)
                group_var(h - 1)
                unit(2 * h + 1, 0, G_hi, G_lo)
                unit(2 * h + 1, 1, G_hi, G_lo)
                retention(h, False)
            j = 2 * RET_HEADS
            unit(j, 0, G_hi, G_lo)
            group_mean(RET_HEADS - 1)
            unit(j, 1, G_hi, G_lo)
            group_var(RET_HEADS - 1)
            pool_product(0)
            unit(j + 1, 0, G_hi, G_lo)
            pool_product(1)
            unit(j + 1, 1, G_hi, G_lo)
            pool_product(2)
            pool_product(3)
            phase(N_OUT0 // 2, A_hi, A_lo, a_ready, 0)

            def mlp(v, n0, fill):
                mean_of_squares(v)
                with pe.Fori(0, FB) as fb:
                    phase(n0 // 2 + fb * KT, G_hi, G_lo, g_ready, KT * v)
                    phase((n0 + KT) // 2 + fb * KT, A_hi, A_lo, a_ready, KT * fill + fb * KT)

            mlp(1, N_MLP0, 1)

            def scores(g, tile):
                t, a = tile // 2, tile % 2
                w = min(BAND, P * (t + 1))
                if tile >= 2:
                    pe.wait_ge(negm_ready, g * (2 * QT) + (tile - 1))
                for c in range(0, w, HALF):
                    n = min(HALF, w - c)
                    last = pe.matmul(PMf[:, 2 * HALF * a + c:2 * HALF * a + c + n],
                                     qT[DH * a:DH * (a + 1), P * t:P * (t + 1)],
                                     kT[DH * a:DH * (a + 1), P * (t + 1) - w + c:P * (t + 1) - w + c + n],
                                     start=True, stop=True)
                last.then_inc(s_done, 1)

            def attention(g, n):
                pe.wait_ge(unit_read, n - 1)
                scores(g, 0)
                scores(g, 1)
                pe.wait_ge(unit_read, n)
                for c in range(QT):
                    last = pe.transpose(PUf[:, P * c:P * (c + 1)], vT[:, P * c:P * (c + 1)], ident)
                last.then_inc(av_turned, 1)
                pe.wait_ge(av_ready, g + 1)
                for tile in range(2 * QT):
                    t, a = tile // 2, tile % 2
                    w = min(BAND, P * (t + 1))
                    at = g * (2 * QT) + tile
                    pe.wait_ge(exp_done, at + 1)
                    for b in range(w // P):
                        last = pe.transpose(PUf[:, P * b:P * (b + 1)], T[:, a, P * b:P * (b + 1)], ident)
                    last.then_inc(pt_done, 1)
                    if tile + 2 < 2 * QT:
                        scores(g, tile + 2)
                    pe.wait_ge(pt_ready, at + 1)
                    if tile >= 2:
                        pe.wait_ge(o_free, at - 1)
                    for b in range(w // P):
                        last = pe.matmul(PU[:, 2 + a, 0:DH], T[:, 2 + a, P * b:P * (b + 1)],
                                         V[:, P * (t + 1 + b) - w + DH * a:P * (t + 1 + b) - w + DH * (a + 1)],
                                         start=(b == 0), stop=(b == w // P - 1))
                    last.then_inc(o_done, 1)
                pe.wait_ge(o_free, g * (2 * QT) + 2 * QT)

            def turn_output(g):
                for t in range(QT):
                    last = pe.transpose(PMf[:, P * t:P * (t + 1)], O_sb[:, t, :], ident)
                last.then_inc(ot_done, 1)

            mean_of_squares(2)
            j = N_ATT // 2
            unit(j, 0, G_hi, G_lo, g_ready, 2 * KT)
            unit(j, 1, G_hi, G_lo)
            unit(j + 1, 0, G_hi, G_lo)
            attention(0, N_ATT + 3)
            with pe.Fori(0, ATT_GROUPS // 2 - 1) as i:
                for b in (1, 2):
                    g = 2 * i + b
                    for u in range(3):
                        n = 3 * b + u
                        unit(j + 3 * i + n // 2, n % 2, G_hi, G_lo)
                        if u == 0:
                            turn_output(g - 1)
                    pe.wait_ge(a_ready, KT * (FB + 1) + g)
                    attention(g, N_ATT + 3 * b + 3 + 6 * i)
            g = ATT_GROUPS - 1
            for u in range(3):
                n = 3 * g + u
                unit(j + n // 2, n % 2, G_hi, G_lo)
                if u == 0:
                    turn_output(g - 1)
            pe.wait_ge(a_ready, KT * (FB + 1) + g)
            attention(g, N_ATT + 3 * g + 3)
            turn_output(g)
            phase(N_OUT1 // 2, A_hi, A_lo, a_ready, KT * (FB + 1))
            mlp(3, N_MLP1, FB + 2)
            mean_of_squares(4)

        @block.scalar
        def _(act):
            chain = Chain(act, act_step)

            def split_w(j, s):
                if isinstance(j, int) and 2 * j + s >= N_UNITS:
                    return
                act.wait_ge(raw_landed[s], 16 * j + 16)
                if not (isinstance(j, int) and j == 0):
                    act.wait_ge(unit_done, 2 * j + s - 1)
                act.copy(W_hi[:, s, :, :].rearrange("p k n -> p (k n)"), raw[:, s, :]).then_inc(w_hi, 1)

            def split_g(v, m):
                act.wait_ge(g_src, KT * v + m + 1)
                act.copy(G_hi[:, m, :], T[:, m % 2, :]).then_inc(g_hi, 1)

            def square_x(v, m):
                if m >= 2:
                    act.wait_ge(ss_added, KT * v + m - 1)
                act.activation(T[:, 2 + m % 2, :], X[:, m, :], ACT.Square).then_inc(sq_ready, 1)

            def root(v):
                act.wait_ge(stat_done, v + 1)
                act.activation(R[:, :], PMf[:, 0:S], ACT.Sqrt, bias=eps[:, 0:1]).then_inc(sd_ready, 1)

            def split_a(at, src, m):
                act.wait_ge(a_src, at + 1)
                act.copy(A_hi[:, m, :], src).then_inc(a_hi, 1)

            split_w(0, 0)
            for m in range(KT):
                split_g(0, m)
                if m == 1:
                    split_w(0, 1)
            act.wait_ge(const_set, 1)
            for m in range(KT):
                square_x(0, m)
            root(0)

            def gn_square(h):
                act.wait_ge(gn_centered, h + 1)
                act.activation(sq_head, OT, ACT.Square).then_inc(gn_sq, 1)

            def gn_root(h):
                act.wait_ge(gn_var, h + 1)
                act.activation(T[:, 3, :], PMf[:, S:2 * S], ACT.Sqrt, bias=eps[:, 1:2]).then_inc(gn_sd, 1)
                act.wait_ge(a_src, h + 1)
                act.copy(A_hi[:, bass.ds(h, 1), :], T[:, 3:4, :]).then_inc(a_hi, 1)

            def head(h, first):
                split_w(2 * h + 1, 0)
                if not first:
                    gn_square(h - 1)
                split_w(2 * h + 1, 1)
                if not first:
                    gn_root(h - 1)
                split_w(2 * h + 2, 0)
                split_w(2 * h + 2, 1)
                act.wait_ge(v_turned, h + 1)
                act.copy(V, PMf[:, 0:S]).then_inc(v_ready, 1)
                act.wait_ge(unit_read, 4 * h + 4)
                act.activation(T[:, 3, :], gate, ACT.Exp, scale=-1.0).then_inc(gate_exp, 1)
                for half in (0, 1):
                    act.wait_ge(pv_done, h * N_RET + (4 if half == 0 else N_RET))
                    act.copy(OT[:, HALF * half:HALF * (half + 1)], PM[:, 3, :]).then_inc(o_evac, 1)

            head(0, True)
            with act.Fori(1, RET_HEADS) as h:
                head(h, False)
            j = 2 * RET_HEADS
            split_w(j + 1, 0)
            gn_square(RET_HEADS - 1)
            split_w(j + 1, 1)
            gn_root(RET_HEADS - 1)
            for i in range(POOL_GROUPS):
                if i < 2:
                    split_w(j + 2, i)
                split_a(RET_HEADS + i, T[:, 2, :], RET_HEADS + i)

            def finish_norm(v, j0):
                for m in range(KT):
                    split_w(j0 + 1 + m // 2, m % 2)
                    if v < 4:
                        split_g(v, m)
                    else:
                        act.wait_ge(unit_read, 2 * j0 + m + 1)
                    square_x(v, m)
                root(v)

            def mlp_in(n0, fill, fb):
                per = 2
                with act.Fori(0, KT // 2) as i:
                    outer = chain.enter(i, per)
                    for s in (0, 1):
                        act.wait_ge(unit_read, n0 + fb * (2 * KT) + 2 * i + (s + 1))
                        chain.link(act.activation(T[:, 2 + s, :], T[:, s, :], ACT.Square))
                        act.copy(A_hi[:, bass.ds(2 * i + s, 1), :], T[:, 2 + s:3 + s, :]).then_inc(a_hi, 1)
                        split_w(n0 // 2 + fb * KT + i + 1, s)
                    chain.leave(outer, per, KT // 2)

            def mlp(v, n0, fill):
                per = KT
                with act.Fori(0, FB - 1) as fb:
                    outer = chain.enter(fb, per)
                    mlp_in(n0, fill, fb)
                    with act.Fori(0, KT // 2) as i:
                        for s in (0, 1):
                            split_w((n0 + KT) // 2 + fb * KT + i + 1, s)
                    chain.leave(outer, per, FB - 1)
                mlp_in(n0, fill, FB - 1)
                finish_norm(v, (n0 + KT) // 2 + (FB - 1) * KT)

            finish_norm(1, N_OUT0 // 2)
            mlp(2, N_MLP0, 1)

            def exp_tile(g, tile):
                t, a = tile // 2, tile % 2
                w = min(BAND, P * (t + 1))
                act.wait_ge(negm_ready, g * (2 * QT) + (tile + 1))
                act.activation(T[:, a, 0:w], T[:, a, 0:w], ACT.Exp, bias=row[:, 16 + tile:17 + tile],
                               accum_out=row[:, 32 + tile:33 + tile]).then_inc(exp_done, 1)

            def attention(g):
                act.wait_ge(av_turned, g + 1)
                act.copy(V, PUf[:, 0:S]).then_inc(av_ready, 1)
                exp_tile(g, 0)
                for tile in range(2 * QT):
                    t, a = tile // 2, tile % 2
                    w = min(BAND, P * (t + 1))
                    if tile + 1 < 2 * QT:
                        exp_tile(g, tile + 1)
                    act.wait_ge(pt_done, g * (2 * QT) + (tile + 1))
                    act.copy(T[:, 2 + a, 0:w], PUf[:, 0:w]).then_inc(pt_ready, 1)

            def output_hi(g):
                act.wait_ge(ot_done, g + 1)
                act.copy(A_hi[:, bass.ds(g, 1), :] if not isinstance(g, int) else A_hi[:, g, :],
                         PMf[:, 0:S] if isinstance(g, int) else
                         PMf[:, 0:S].rearrange("p (o n) -> p o n", o=1)).then_inc(a_hi, 1)

            j = N_ATT // 2
            for u in range(3):
                split_w(j + (u + 2) // 2, u % 2)
            attention(0)
            with act.Fori(0, ATT_GROUPS // 2 - 1) as i:
                for b in (1, 2):
                    g = 2 * i + b
                    for u in range(3):
                        n = 3 * b + u
                        split_w(j + 3 * i + (n + 2) // 2, n % 2)
                        if u == 0:
                            output_hi(g - 1)
                    attention(g)
            g = ATT_GROUPS - 1
            for u in range(3):
                n = 3 * g + u
                split_w(j + (n + 2) // 2, n % 2)
                if u == 0:
                    output_hi(g - 1)
            attention(g)
            output_hi(g)
            finish_norm(3, N_OUT1 // 2)
            mlp(4, N_MLP1, FB + 2)

        @block.vector
        def _(dve):
            chain = Chain(dve, dve_step)
            link = chain.link

            def banks(s):
                return PUf[:, S * s:S * (s + 1)]

            def split_w(j, s):
                if isinstance(j, int) and 2 * j + s >= N_UNITS:
                    return
                dve.wait_ge(w_hi, 2 * j + s + 1)
                dve.tensor_tensor(W_lo[:, s, :, :].rearrange("p k n -> p (k n)"), raw[:, s, :],
                                  W_hi[:, s, :, :].rearrange("p k n -> p (k n)").bitcast(F32),
                                  ALU.subtract).then_inc(w_lo, 1)

            def scale_g(v, m):
                at = C_GAIN + KT * v + m
                if m >= 2:
                    dve.wait_ge(g_ready, KT * v + m - 1)
                dve.tensor_scalar(T[:, m % 2, :], X[:, m, :], C[:, at:at + 1], None, ALU.mult).then_inc(g_src, 1)

            def split_g(v, m):
                dve.wait_ge(g_hi, KT * v + m + 1)
                dve.tensor_tensor(G_lo[:, m, :], T[:, m % 2, :], G_hi[:, m, :].bitcast(F32),
                                  ALU.subtract).then_inc(g_ready, 1)

            def add_squares(v, m):
                dve.wait_ge(sq_ready, KT * v + m + 1)
                if m == 0:
                    dve.tensor_copy(R[:, :], T[:, 2, :]).then_inc(ss_added, 1)
                else:
                    dve.wait_ge(ss_added, KT * v + m)
                    dve.tensor_tensor(R[:, :], R[:, :], T[:, 2 + m % 2, :], ALU.add).then_inc(ss_added, 1)

            def inverse_root(v):
                dve.wait_ge(sd_ready, v + 1)
                dve.reciprocal(R[:, :], R[:, :]).then_inc(r_ready, 1)
                dve.wait_ge(r_ready, v + 1)

            def done(j, s):
                dve.wait_ge(unit_done, 2 * j + s + 1)

            dve.memset(ones_d[:, :], 1.0 / D)
            dve.memset(ones_h[:, :], 1.0 / P)
            dve.memset(row[:, 94:95], 0.0)
            dve.memset(eps[:, 0:1], RMS_EPS)
            dve.memset(eps[:, 1:2], GN_EPS).then_inc(const_set, 1)
            dve.wait_ge(const_landed, 16)
            split_w(0, 0)
            for m in range(KT + 1):
                if m < KT:
                    dve.wait_ge(x_landed[m], 16)
                    scale_g(0, m)
                if m >= 1:
                    split_g(0, m - 1)
                if m == 2:
                    split_w(0, 1)
            for m in range(KT):
                add_squares(0, m)
            inverse_root(0)
            dve.wait_ge(rot_landed, 16)
            link(dve.tensor_tensor(cosR, cosR, R[:, :], ALU.mult))
            link(dve.tensor_tensor(sinR, sinR, R[:, :], ALU.mult))

            def rotate(j, s, dst):
                done(j, s)
                if not (isinstance(j, int) and j + s == 0):
                    dve.wait_ge(rotated, j + s)
                dve.tensor_tensor(dst, banks(s), cosR, ALU.mult)
                dve.tensor_tensor(T[0:64, 2, :], banks(s)[64:128], sinR[0:64], ALU.mult)
                ins = dve.tensor_tensor(T[64:128, 2, :], banks(s)[0:64], sinR[64:128], ALU.mult)
                ins.then_inc(unit_read, 1)
                dve.wait_ge(unit_read, 2 * j + s + 1)
                dve.tensor_tensor(dst, dst, T[:, 2, :], ALU.add).then_inc(rotated, 1)

            def gn_center(h):
                dve.wait_ge(gn_mean, h + 1)
                dve.tensor_tensor(OT, OT, PMf[:, 0:S], ALU.subtract).then_inc(gn_centered, 1)

            def gn_scale(h):
                dve.wait_ge(gn_sd, h + 1)
                link(dve.reciprocal(T[:, 3, :], T[:, 3, :]))
                link(dve.tensor_tensor(T[:, 3, :], T[:, 3, :], OT, ALU.mult))
                gain = C[:, C_GN + h:C_GN + h + 1] if isinstance(h, int) else C[:, bass.ds(h + C_GN, 1)]
                dve.scalar_tensor_tensor(out=T[:, 3, :], in0=T[:, 3, :], scalar=gain, in1=gate, op0=ALU.mult,
                                         op1=ALU.mult).then_inc(a_src, 1)
                dve.wait_ge(a_hi, h + 1)
                dve.tensor_tensor(A_lo[:, bass.ds(h, 1), :], T[:, 3:4, :], A_hi[:, bass.ds(h, 1), :].bitcast(F32),
                                  ALU.subtract).then_inc(a_ready, 1)

            def head(h, first):
                rotate(2 * h, 0, qT)
                split_w(2 * h + 1, 0)
                if not first:
                    gn_center(h - 1)
                rotate(2 * h, 1, kT)
                split_w(2 * h + 1, 1)
                if not first:
                    gn_scale(h - 1)
                done(2 * h + 1, 0)
                dve.tensor_tensor(vT, banks(0), R[:, :], ALU.mult).then_inc(unit_read, 1)
                split_w(2 * h + 2, 0)
                done(2 * h + 1, 1)
                dve.tensor_tensor(gate, banks(1), R[:, :], ALU.mult).then_inc(unit_read, 1)
                split_w(2 * h + 2, 1)
                dve.wait_ge(dec_landed, 16 * h + 16)
                for x, (q0, n, kt) in enumerate(RET_STEPS):
                    dve.wait_ge(score_done, h * N_RET + (x + 1))
                    if x >= 3:
                        dve.wait_ge(pv_done, h * N_RET + (x - 2))
                    dve.tensor_tensor(probs[x % 3][:, 0:n], PM[:, x % 3, 0:n],
                                      dec[:, q0 - P * kt:q0 - P * kt + n], ALU.mult).then_inc(p_ready, 1)
                dve.wait_ge(gate_exp, h + 1)
                link(dve.tensor_scalar(T[:, 3, :], T[:, 3, :], 1.0, None, ALU.add))
                link(dve.reciprocal(T[:, 3, :], T[:, 3, :]))
                link(dve.tensor_tensor(gate, gate, T[:, 3, :], ALU.mult))

            head(0, True)
            with dve.Fori(1, RET_HEADS) as h:
                outer = chain.enter(h - 1, 5)
                head(h, False)
                chain.leave(outer, 5, RET_HEADS - 1)

            def pool_window(j, s, i):
                done(j, s)
                if i:
                    dve.wait_ge(pooled, i)
                tok = X[:, 0, :]
                ins = dve.tensor_tensor(tok, banks(s), R[:, :], ALU.mult)
                ins.then_inc(unit_read, 1)
                dve.wait_ge(unit_read, 2 * j + s + 1)
                cur = tok
                for step in range(i + 1):
                    lag = 1 << step
                    nxt = X[:, 1 if step % 2 == 0 else 3, :]
                    dve.tensor_copy(nxt[:, 0:lag], cur[:, 0:lag])
                    link(dve.tensor_tensor(nxt[:, lag:S], cur[:, lag:S], cur[:, 0:S - lag], ALU.add))
                    cur = nxt
                y = X[:, 6 + i % 2, :]
                cnt = C[:, C_CNT + EDGE * i:C_CNT + EDGE * (i + 1)]
                link(dve.tensor_tensor(y[:, 0:EDGE], cur[:, 0:EDGE], cnt, ALU.mult))
                dve.tensor_tensor(y[:, 0:EDGE], y[:, 0:EDGE], tok[:, 0:EDGE], ALU.subtract)
                dve.scalar_tensor_tensor(out=y[:, EDGE:S], in0=cur[:, EDGE:S], scalar=1.0 / POOL_WINDOWS[i],
                                         in1=tok[:, EDGE:S], op0=ALU.mult, op1=ALU.subtract).then_inc(pooled, 1)

            def pool_scale(i):
                dve.wait_ge(pool_mm, i + 1)
                dve.wait_ge(a_ready, RET_HEADS + i)
                dve.tensor_scalar(T[:, 2, :], PMf[:, S * (i % 2):S * (i % 2 + 1)], C[:, C_PS + i:C_PS + i + 1],
                                  None, ALU.mult).then_inc(a_src, 1)
                at = RET_HEADS + i
                dve.wait_ge(a_hi, at + 1)
                dve.tensor_tensor(A_lo[:, at, :], T[:, 2, :], A_hi[:, at, :].bitcast(F32),
                                  ALU.subtract).then_inc(a_ready, 1)

            j = 2 * RET_HEADS
            pool_window(j, 0, 0)
            split_w(j + 1, 0)
            gn_center(RET_HEADS - 1)
            pool_window(j, 1, 1)
            split_w(j + 1, 1)
            gn_scale(RET_HEADS - 1)
            pool_window(j + 1, 0, 2)
            split_w(j + 2, 0)
            pool_scale(0)
            pool_window(j + 1, 1, 3)
            split_w(j + 2, 1)
            pool_scale(1)
            pool_scale(2)
            pool_scale(3)

            def add_unit(j, s, m):
                done(j, s)
                x = X[:, m, :] if isinstance(m, int) else X[:, bass.ds(m, 1), :]
                src = banks(s) if isinstance(m, int) else banks(s).rearrange("p (o n) -> p o n", o=1)
                return dve.tensor_tensor(x, x, src, ALU.add)

            def finish_norm(v, j0, landed=0):
                for m in range(KT):
                    if landed:
                        dve.wait_ge(x_landed[m], landed)
                    add_unit(j0 + m // 2, m % 2, m).then_inc(unit_read, 1)
                    dve.wait_ge(unit_read, 2 * j0 + m + 1)
                    if v < 4:
                        scale_g(v, m)
                        split_g(v, m)
                    split_w(j0 + 1 + m // 2, m % 2)
                    add_squares(v, m)
                inverse_root(v)

            def mlp_in(n0, fill, fb):
                with dve.Fori(0, KT // 2) as i:
                    for s in (0, 1):
                        j = n0 // 2 + fb * KT + i
                        at = KT * fill + fb * KT + 2 * i + s
                        done(j, s)
                        dve.scalar_tensor_tensor(out=T[:, s, :], in0=banks(s), scalar=0.0, in1=R[:, :], op0=ALU.max,
                                                 op1=ALU.mult).then_inc(unit_read, 1)
                        dve.wait_ge(a_hi, at + 1)
                        dve.tensor_tensor(A_lo[:, bass.ds(2 * i + s, 1), :], T[:, 2 + s:3 + s, :],
                                          A_hi[:, bass.ds(2 * i + s, 1), :].bitcast(F32),
                                          ALU.subtract).then_inc(a_ready, 1)
                        split_w(j + 1, s)

            def mlp(v, n0, fill):
                with dve.Fori(0, FB - 1) as fb:
                    mlp_in(n0, fill, fb)
                    with dve.Fori(0, KT // 2) as i:
                        for s in (0, 1):
                            j = (n0 + KT) // 2 + fb * KT + i
                            add_unit(j, s, 2 * i + s).then_inc(unit_read, 1)
                            split_w(j + 1, s)
                mlp_in(n0, fill, FB - 1)
                finish_norm(v, (n0 + KT) // 2 + (FB - 1) * KT)

            finish_norm(1, N_OUT0 // 2, landed=32)
            mlp(2, N_MLP0, 1)
            dve.wait_ge(spilled, 16 * KT)

            def normalise(g, tile):
                t, a = tile // 2, tile % 2
                at = g * (2 * QT) + tile
                dve.wait_ge(exp_done, at + 1)
                link(dve.reciprocal(row[:, 48 + tile:49 + tile], row[:, 32 + tile:33 + tile]))
                dve.wait_ge(o_done, at + 1)
                dve.tensor_scalar(O_sb[:, t, DH * a:DH * (a + 1)], PU[:, 2 + a, 0:DH], row[:, 48 + tile:49 + tile],
                                  None, ALU.mult).then_inc(o_free, 1)

            def attention(g):
                dve.wait_ge(b_masked, 4)
                dve.wait_ge(b_ready, g * 8 + 8)
                for tile in range(2 * QT):
                    t, a = tile // 2, tile % 2
                    w = min(BAND, P * (t + 1))
                    at = g * (2 * QT) + tile
                    if tile >= 2:
                        dve.wait_ge(pt_done, at - 1)
                    dve.wait_ge(s_done, at + 1)
                    dve.memset(row[:, 95:96], 0.0)
                    link(dve.tensor_tensor_reduce(T[:, a, 0:w], PMf[:, S * a:S * a + w], bias[:, a, BAND - w:BAND], 1.0,
                                                  -3.0e38, ALU.add, ALU.max, row[:, tile:tile + 1]))
                    dve.tensor_scalar(row[:, 16 + tile:17 + tile], row[:, tile:tile + 1], -1.0, None,
                                      ALU.mult).then_inc(negm_ready, 1)
                    if tile >= 2:
                        normalise(g, tile - 2)
                normalise(g, 2 * QT - 2)
                normalise(g, 2 * QT - 1)

            def output_lo(g):
                dve.wait_ge(a_hi, KT * (FB + 1) + g + 1)
                dve.tensor_tensor(A_lo[:, bass.ds(g, 1), :], PMf[:, 0:S].rearrange("p (o n) -> p o n", o=1),
                                  A_hi[:, bass.ds(g, 1), :].bitcast(F32), ALU.subtract).then_inc(a_ready, 1)

            def att_unit(j, u, s, g):
                done(j, s)
                if u == 0:
                    dve.scalar_tensor_tensor(out=qT, in0=banks(s), scalar=DH ** -0.5, in1=R[:, :], op0=ALU.mult,
                                             op1=ALU.mult).then_inc(unit_read, 1)
                else:
                    dve.tensor_tensor(kT if u == 1 else vT, banks(s), R[:, :], ALU.mult).then_inc(unit_read, 1)
                split_w(j + 1, s)

            j = N_ATT // 2
            per = 4 * QT
            for u in range(3):
                att_unit(j + u // 2, u, u % 2, 0)
            attention(0)
            with dve.Fori(0, ATT_GROUPS // 2 - 1) as i:
                outer = chain.enter(i, 2 * per)
                for b in (1, 2):
                    g = 2 * i + b
                    for u in range(3):
                        n = 3 * b + u
                        att_unit(j + 3 * i + n // 2, u, n % 2, g)
                        if u == 0:
                            output_lo(g - 1)
                    attention(g)
                chain.leave(outer, 2 * per, ATT_GROUPS // 2 - 1)
            g = ATT_GROUPS - 1
            for u in range(3):
                n = 3 * g + u
                att_unit(j + n // 2, u, n % 2, g)
                if u == 0:
                    output_lo(g - 1)
            attention(g)
            output_lo(g)
            finish_norm(3, N_OUT1 // 2, landed=48)
            mlp(4, N_MLP1, FB + 2)
            for m in range(KT):
                at = C_GAIN + KT * 4 + m
                dve.scalar_tensor_tensor(out=X[:, m, :], in0=X[:, m, :], scalar=C[:, at:at + 1], in1=R[:, :],
                                         op0=ALU.mult, op1=ALU.mult).then_inc(y_ready, 1)


def _units(w):
    rows, cols = w.shape[0] // D, w.shape[1] // P
    return w.reshape(rows, KT, P, cols, P).transpose(0, 3, 2, 1, 4).reshape(rows * cols, P, D)


def _tables():
    import numpy as np
    f = np.float32
    half = P // 2
    inv_freq = f(1.0) / np.power(f(10000.0), np.linspace(0.0, 1.0, half, dtype=f), dtype=f)
    ang = (np.arange(S, dtype=f)[:, None] * inv_freq[None, :]).astype(f).T
    cos, sin = np.cos(ang.astype(np.float64)), np.sin(ang.astype(np.float64))
    rot = np.stack([np.concatenate([cos, cos]), np.concatenate([-sin, sin])], 1).astype(f)
    p, c = np.arange(P)[:, None], np.arange(S)[None, :]
    log_g = np.log1p(-np.exp2(-5.0 - np.arange(RET_HEADS)))
    decay = np.exp(np.abs(c - p)[None] * log_g[:, None, None])
    decay = np.where(c // DH < p // DH, 0.0, decay) * P ** -0.5
    tokens = np.arange(EDGE) + 1
    cnt = np.concatenate([1.0 / np.minimum(tokens, w) for w in POOL_WINDOWS])
    return rot, decay.astype(f), cnt.astype(f)


def kernel(x, mix_norm, ffn_norm, w_ffn_in, w_ffn_out, ab_w_in, ab_gn_gain, ab_w_pool, ab_pool_scale, ab_w_out,
           c_w_qkv, c_rel_bias, c_w_out, final_norm):
    import numpy as np
    import concourse.bacc as bacc
    from concourse.bass_utils import run_bass_kernel_spmd

    (x, mix_norm, ffn_norm, w_ffn_in, w_ffn_out, ab_w_in, ab_gn_gain, ab_w_pool, ab_pool_scale, ab_w_out, c_w_qkv,
     c_rel_bias, c_w_out, final_norm) = map(np.asarray, (
         x, mix_norm, ffn_norm, w_ffn_in, w_ffn_out, ab_w_in, ab_gn_gain, ab_w_pool, ab_pool_scale, ab_w_out, c_w_qkv,
         c_rel_bias, c_w_out, final_norm))

    ret = RET_HEADS * P
    w_in = ab_w_in[0]
    turned = np.concatenate([np.arange(0, P, 2), np.arange(1, P, 2)])
    parts = []
    for h in range(RET_HEADS):
        for part in range(4):
            w = w_in[:, part * ret + h * P:part * ret + (h + 1) * P]
            parts.append(_units(w[:, turned] if part < 2 else w))
    parts += [_units(w_in[:, 4 * ret:]), _units(ab_w_out[0])]

    def mlp(layer):
        for fb in range(FB):
            parts.append(_units(w_ffn_in[layer][:, fb * D:(fb + 1) * D]))
            parts.append(_units(w_ffn_out[layer][fb * D:(fb + 1) * D]))

    mlp(0)
    for g in range(ATT_GROUPS):
        parts.extend(_units(c_w_qkv[0][:, part * D + g * P:part * D + (g + 1) * P]) for part in range(3))
    parts.append(_units(c_w_out[0]))
    mlp(1)
    weights = np.concatenate(parts)

    rot, decay, cnt = _tables()
    norms = [mix_norm[0], ffn_norm[0], mix_norm[1], ffn_norm[1], final_norm]
    small = np.concatenate(
        [np.eye(P, dtype=np.float32)] + [g.reshape(KT, P).T for g in norms]
        + [ab_gn_gain[0].reshape(RET_HEADS, P).T, ab_pool_scale[0].reshape(POOL_GROUPS, P).T,
           np.broadcast_to(cnt, (P, cnt.size))], axis=1)
    n_rel = c_rel_bias.shape[-1]
    rel = c_rel_bias[0][:, np.minimum(1 + np.arange(REL_ROW), n_rel - 1)]
    arrays = {
        "weights": weights,
        "x_in": x[0].T.reshape(KT, P, S),
        "small": small,
        "rot": rot,
        "decay": decay,
        "w_pool": ab_w_pool[0].transpose(1, 0, 2).reshape(P, POOL_GROUPS * P),
        "rel": rel,
    }
    arrays = {name: np.ascontiguousarray(a) for name, a in arrays.items()}
    nc = bacc.Bacc("TRN2", target_bir_lowering=False, num_devices=1)
    args = [nc.dram_tensor(name, a.shape, F32, kind="ExternalInput").ap() for name, a in arrays.items()]
    out = nc.dram_tensor("out", (KT, P, S), F32, kind="ExternalOutput").ap()
    spill = nc.dram_tensor("spill", (KT, P, S), F32).ap()
    trunk_kernel(nc, *args, out, spill)
    result = run_bass_kernel_spmd(nc, [arrays], core_ids=[0]).results[0]["out"]
    return np.ascontiguousarray(result.reshape(D, S).T)[None]
```

```python
from contextlib import ExitStack

import concourse.bass as bass
from concourse import mybir

P = 128
D = 1024
S = 1024
KT = D // P
HALF = 512
FB = 4
RET_HEADS = 4
POOL_WINDOWS = (2, 4, 8, 16)
POOL_GROUPS = len(POOL_WINDOWS)
EDGE = POOL_WINDOWS[-1]
ATT_GROUPS = 8
DH = 64
QT = S // P
BAND = 640
REL = 256
REL_ROW = 383
RMS_EPS = 1e-6
GN_EPS = 1e-5
MASKED = -1e30

N_OUT0 = 4 * RET_HEADS + POOL_GROUPS
N_MLP0 = N_OUT0 + KT
N_ATT = N_MLP0 + 2 * KT * FB
N_OUT1 = N_ATT + 3 * ATT_GROUPS
N_MLP1 = N_OUT1 + KT
N_UNITS = N_MLP1 + 2 * KT * FB

RET_STEPS = [(max(HALF * half, P * j), HALF * (half + 1) - max(HALF * half, P * j), j)
             for half in (0, 1) for j in range(4 * (half + 1))]
N_RET = len(RET_STEPS)

C_ID = 0
C_GAIN = C_ID + P
C_GN = C_GAIN + 5 * KT
C_PS = C_GN + RET_HEADS
C_CNT = C_PS + POOL_GROUPS
C_ALL = C_CNT + POOL_GROUPS * EDGE

F32 = mybir.dt.float32
F32R = mybir.dt.float32r
ALU = mybir.AluOpType
ACT = mybir.ActivationFunctionType


class Chain:

    def __init__(self, eng, sem):
        self.eng, self.sem, self.base, self.k = eng, sem, 0, 0

    def link(self, ins):
        ins.then_inc(self.sem, 1)
        self.k += 1
        self.eng.wait_ge(self.sem, self.base + self.k)

    def enter(self, i, per):
        outer = (self.base, self.k)
        self.base, self.k = self.base + self.k + i * per, 0
        return outer

    def leave(self, outer, per, count):
        assert self.k == per, (self.k, per)
        self.base, self.k = outer[0], outer[1] + per * count


def trunk_kernel(nc, weights, x_in, small, rot, decay, w_pool, rel, out, spill):
    with ExitStack() as ctx:
        def sb(name, shape, dt=F32):
            return ctx.enter_context(nc.sbuf_tensor(name, shape, dt))

        def sem(name):
            return ctx.enter_context(nc.semaphore(name))

        def next_place():
            return (nc.sbuf_base + 31) // 32 * 32

        x_at = next_place()
        X = sb("X", [P, KT, S])
        G_hi = sb("G_hi", [P, KT, S], F32R)
        G_lo = sb("G_lo", [P, KT, S], F32R)
        a_at = next_place()
        A_hi = sb("A_hi", [P, KT, S], F32R)
        A_lo = sb("A_lo", [P, KT, S], F32R)
        raw = sb("raw", [P, 2, S])
        W_hi = sb("W_hi", [P, 2, KT, P], F32R)
        W_lo = sb("W_lo", [P, 2, KT, P], F32R)
        R = sb("R", [P, S])
        t_at = next_place()
        T = sb("T", [P, 4, S])
        C = sb("C", [P, C_ALL])
        ones_d = sb("ones_d", [P, P])
        ones_h = sb("ones_h", [P, P])
        eps = sb("eps", [P, 2])
        row = sb("row", [P, 6 * 16])

        PU = ctx.enter_context(nc.psum_tensor("PU", [P, 4, HALF], F32))
        PM = ctx.enter_context(nc.psum_tensor("PM", [P, 4, HALF], F32))
        PUf = PU[:, :, :].rearrange("p b n -> p (b n)")
        PMf = PM[:, :, :].rearrange("p b n -> p (b n)")

        qT, kT, vT, V, gate = X[:, 0, :], X[:, 1, :], X[:, 2, :], X[:, 3, :], X[:, 4, :]
        OT = X[:, 2, :]
        Xf = X[:, :, :].rearrange("p k n -> p (k n)")
        probs = [Xf[:, 5 * S + HALF * i:5 * S + HALF * (i + 1)] for i in range(3)]
        sq_head = X[:, 5, :]
        dec = X[:, 7, :]
        cosR, sinR = T[:, 0, :], T[:, 1, :]
        O_sb = X[:, 7, :].rearrange("p (t f) -> p t f", t=QT)
        WP = X[:, 4, :]
        ident = C[:, C_ID:C_ID + P]

        def alias(name, shape, dt, offset):
            return nc.alloc_sbuf_tensor_at(name, shape, dt, offset=offset)

        Q_s = [alias(f"Q_s{a}", [P, S], F32R, x_at + 4 * S * a) for a in (0, 1)]
        K_s = [alias(f"K_s{a}", [P, S], F32R, x_at + 4 * S * (2 + a)) for a in (0, 1)]
        K_lo = alias("K_lo", [P, S], F32R, x_at + 4 * S * 4)
        VV = alias("VV", [P, QT, 2 * P], F32R, x_at + 4 * S * 5)
        PT = alias("PT", [P, 2, 2, BAND], F32R, t_at + 4 * 2 * BAND)
        B = [alias(f"B{a}", [P, S], F32, a_at + 4 * S * (KT * (a + 1) - 1)) for a in (0, 1)]
        bias = [B[a][:, 0:BAND] for a in (0, 1)]
        rel_t = [B[a][:, BAND:BAND + REL] for a in (0, 1)]
        Tf = T[:, :, :].rearrange("p k n -> p (k n)")
        prob = [Tf[:, BAND * a:BAND * (a + 1)] for a in (0, 1)]
        turned = [PUf[:, S * a:S * a + BAND] for a in (0, 1)]
        O_ps = [PM[:, 2 + a, 0:2 * P] for a in (0, 1)]
        q_in, k_in, v_in = Tf[:, 0:S], Tf[:, 2 * BAND:2 * BAND + S], Tf[:, 2 * BAND + S:2 * BAND + 2 * S]

        raw_landed = [sem("raw_landed0"), sem("raw_landed1")]
        w_hi, w_lo = sem("w_hi"), sem("w_lo")
        unit_done = sem("unit_done")
        unit_read = sem("unit_read")
        g_src, g_hi, g_ready = sem("g_src"), sem("g_hi"), sem("g_ready")
        a_src, a_hi, a_ready = sem("a_src"), sem("a_hi"), sem("a_ready")
        sq_ready, ss_added = sem("sq_ready"), sem("ss_added")
        stat_done, sd_ready, r_ready = sem("stat_done"), sem("sd_ready"), sem("r_ready")
        x_landed = [sem(f"x_landed{m}") for m in range(KT)]
        const_landed, const_set = sem("const_landed"), sem("const_set")
        rot_landed, dec_landed, wp_landed = sem("rot_landed"), sem("dec_landed"), sem("wp_landed")
        rotated, v_turned, v_ready = sem("rotated"), sem("v_turned"), sem("v_ready")
        gate_exp = sem("gate_exp")
        score_done, p_ready, pv_done, o_evac = sem("score_done"), sem("p_ready"), sem("pv_done"), sem("o_evac")
        gn_mean, gn_centered, gn_sq, gn_var, gn_sd = (sem("gn_mean"), sem("gn_centered"), sem("gn_sq"),
                                                      sem("gn_var"), sem("gn_sd"))
        pooled, pool_mm = sem("pooled"), sem("pool_mm")
        spilled = sem("spilled")
        qk_hi, qk_ready = sem("qk_hi"), sem("qk_ready")
        av_turned, av_hi, av_ready = sem("av_turned"), sem("av_hi"), sem("av_ready")
        b_masked, b_landed, b_ready = sem("b_masked"), sem("b_landed"), sem("b_ready")
        s_done, negm_ready, exp_done, pt_done, pt_hi, pt_ready, o_done, o_free, ot_done = (
            sem("s_done"), sem("negm_ready"), sem("exp_done"), sem("pt_done"), sem("pt_hi"), sem("pt_ready"),
            sem("o_done"), sem("o_free"), sem("ot_done"))
        share_ready = sem("share_ready")
        y_ready, out_landed = sem("y_ready"), sem("out_landed")
        dve_step, act_step = sem("dve_step"), sem("act_step")

        block = ctx.enter_context(nc.Block())

        @block.sync
        def _(sp):
            sp.dma_start(raw[:, 0, :], weights[0]).then_inc(raw_landed[0], 16)
            sp.dma_start(raw[:, 1, :], weights[1]).then_inc(raw_landed[1], 16)
            with sp.Fori(1, N_UNITS // 2) as j:
                for s in (0, 1):
                    sp.wait_ge(w_lo, 2 * j + (s - 1))
                    sp.dma_start(raw[:, s:s + 1, :],
                                 weights[bass.ds(2 * j + s, 1)].rearrange("u p n -> p u n")).then_inc(raw_landed[s], 16)

        @block.gpsimd
        def _(pool):
            pool.dma_start(C[:, :], small).then_inc(const_landed, 16)
            for m in range(KT):
                pool.dma_start(X[:, m, :], x_in[m]).then_inc(x_landed[m], 16)
            pool.wait_ge(r_ready, 1)
            pool.dma_start(T[:, 0:2, :], rot).then_inc(rot_landed, 16)
            pool.dma_start(dec, decay[0]).then_inc(dec_landed, 16)
            with pool.Fori(1, RET_HEADS) as h:
                pool.wait_ge(p_ready, h * N_RET)
                pool.dma_start(X[:, 7:8, :], decay[bass.ds(h, 1)].rearrange("h p n -> p h n")).then_inc(dec_landed, 16)
            pool.wait_ge(a_src, RET_HEADS)
            pool.dma_start(WP[:, 0:POOL_GROUPS * P], w_pool).then_inc(wp_landed, 16)
            pool.wait_ge(a_ready, KT)
            for m in range(KT):
                pool.dma_start(X[:, m, :], x_in[m]).then_inc(x_landed[m], 16)
            for m in range(KT):
                pool.wait_ge(unit_read, N_ATT - KT + m + 1)
                pool.dma_start(spill[m], X[:, m, :]).then_inc(spilled, 16)
            pool.wait_ge(spilled, 16 * KT)
            pool.wait_ge(r_ready, 3)
            for a in (0, 1):
                pool.memset(bias[a][0:DH, BAND - DH:BAND], MASKED).then_inc(b_masked, 1)
                pool.memset(bias[a][DH:P, 0:DH], MASKED).then_inc(b_masked, 1)

            def bias_tiles(g):
                for a in (0, 1):
                    pool.dma_start(rel_t[a], bass.AP(tensor=rel.tensor, offset=g * (2 * REL_ROW) + a * REL_ROW,
                                                     ap=[[1, P], [1, REL]])).then_inc(b_landed, 16)
                pool.wait_ge(b_landed, g * 32 + 32)
                for a in (0, 1):
                    for rows, first, end in ((slice(0, DH), 0, BAND - DH), (slice(DH, P), DH, BAND)):
                        near = rel_t[a][rows, REL - (end - (BAND - REL)):REL][:, ::-1]
                        far = rel_t[a][rows, REL - 1:REL].to_broadcast([DH, BAND - REL - first])
                        zero = row[rows, 94:95]
                        for to, of in ((slice(BAND - REL, end), near), (slice(first, BAND - REL), far)):
                            pool.tensor_tensor(bias[a][rows, to], of, zero.to_broadcast([DH, to.stop - to.start]),
                                               ALU.add).then_inc(b_ready, 1)

            bias_tiles(0)
            with pool.Fori(1, ATT_GROUPS) as g:
                pool.wait_ge(negm_ready, g * (2 * QT))
                bias_tiles(g)
            pool.wait_ge(a_ready, KT * (FB + 2))
            for m in range(KT):
                pool.dma_start(X[:, m, :], spill[m]).then_inc(x_landed[m], 16)
            for m in range(KT):
                pool.wait_ge(y_ready, m + 1)
                pool.dma_start(out[m], X[:, m, :]).then_inc(out_landed, 16)
            pool.wait_ge(out_landed, 16 * KT)

        @block.tensor
        def _(pe):
            def unit(j, s, hi, lo, ready=None, base=0, between=None):
                pe.wait_ge(w_lo, 2 * j + s + 1)
                if not (isinstance(j, int) and j == 0):
                    pe.wait_ge(unit_read, 2 * j + s - 1)
                for k in range(KT):
                    if ready is not None:
                        pe.wait_ge(ready, base + k + 1)
                    if between is not None and k == KT - 2:
                        between()
                    for n, (w, x) in enumerate(((W_hi, hi), (W_hi, lo), (W_lo, hi))):
                        for half in (0, 1):
                            last = pe.matmul(PU[:, 2 * s + half, :], w[:, s, k, :],
                                             x[:, k, HALF * half:HALF * (half + 1)],
                                             start=(k == 0 and n == 0), stop=(k == KT - 1 and n == 2))
                last.then_inc(unit_done, 1)

            def phase(j0, hi, lo, ready, base, pairs=KT // 2):
                unit(j0, 0, hi, lo, ready, base)
                unit(j0, 1, hi, lo)
                with pe.Fori(1, pairs) as i:
                    for s in (0, 1):
                        unit(j0 + i, s, hi, lo)

            def mean_of_squares(v):
                pe.wait_ge(ss_added, KT * (v + 1))
                for half in (0, 1):
                    last = pe.matmul(PM[:, half, :], ones_d[:, :], R[:, HALF * half:HALF * (half + 1)],
                                     start=True, stop=True)
                last.then_inc(stat_done, 1)

            def group_mean(h):
                pe.wait_ge(o_evac, 2 * h + 2)
                for half in (0, 1):
                    last = pe.matmul(PM[:, half, :], ones_h[:, :], OT[:, HALF * half:HALF * (half + 1)],
                                     start=True, stop=True)
                last.then_inc(gn_mean, 1)

            def group_var(h):
                pe.wait_ge(gn_sq, h + 1)
                for half in (0, 1):
                    last = pe.matmul(PM[:, 2 + half, :], ones_h[:, :], sq_head[:, HALF * half:HALF * (half + 1)],
                                     start=True, stop=True)
                last.then_inc(gn_var, 1)

            def retention(h, first):
                pe.wait_ge(unit_read, 4 * h + 3)
                for c in range(QT):
                    last = pe.transpose(PMf[:, P * c:P * (c + 1)], vT[:, P * c:P * (c + 1)], ident)
                last.then_inc(v_turned, 1)
                pe.wait_ge(v_ready, h + 1)
                pe.wait_ge(rotated, 2 * h + 2)
                if not first:
                    pe.wait_ge(gn_sd, h)
                for x in range(N_RET + 3):
                    if x >= 3:
                        y = x - 3
                        q0, n, kt = RET_STEPS[y]
                        pe.wait_ge(p_ready, h * N_RET + (y + 1))
                        if kt == 0 and q0:
                            pe.wait_ge(o_evac, 2 * h + 1)
                        end = kt == (3 if q0 < HALF else 7)
                        pe.matmul(PM[:, 3, q0 % HALF:q0 % HALF + n], V[:, P * kt:P * (kt + 1)], probs[y % 3][:, 0:n],
                                  start=(kt == 0), stop=end).then_inc(pv_done, 1)
                    if x < N_RET:
                        q0, n, kt = RET_STEPS[x]
                        pe.matmul(PM[:, x % 3, 0:n], kT[:, P * kt:P * (kt + 1)], qT[:, q0:q0 + n],
                                  start=True, stop=True).then_inc(score_done, 1)

            def pool_product(i):
                if i == 0:
                    pe.wait_ge(wp_landed, 16)
                pe.wait_ge(pooled, i + 1)
                if i == 1:
                    pe.wait_ge(gn_sd, RET_HEADS)
                if i >= 2:
                    pe.wait_ge(a_src, RET_HEADS + i - 1)
                for half in (0, 1):
                    last = pe.matmul(PM[:, 2 * (i % 2) + half, :], WP[:, P * i:P * (i + 1)],
                                     X[:, 6 + i % 2, HALF * half:HALF * (half + 1)], start=True, stop=True)
                last.then_inc(pool_mm, 1)

            pe.wait_ge(const_landed, 16)
            pe.wait_ge(const_set, 1)
            for s in (0, 1):
                unit(0, s, G_hi, G_lo, g_ready if s == 0 else None)
                if s == 0:
                    mean_of_squares(0)
            for s in (0, 1):
                unit(1, s, G_hi, G_lo)
            retention(0, True)
            with pe.Fori(1, RET_HEADS) as h:
                unit(2 * h, 0, G_hi, G_lo)
                group_mean(h - 1)
                unit(2 * h, 1, G_hi, G_lo)
                group_var(h - 1)
                unit(2 * h + 1, 0, G_hi, G_lo)
                unit(2 * h + 1, 1, G_hi, G_lo)
                retention(h, False)
            j = 2 * RET_HEADS
            unit(j, 0, G_hi, G_lo)
            group_mean(RET_HEADS - 1)
            unit(j, 1, G_hi, G_lo)
            group_var(RET_HEADS - 1)
            pool_product(0)
            unit(j + 1, 0, G_hi, G_lo)
            pool_product(1)
            unit(j + 1, 1, G_hi, G_lo)
            pool_product(2)
            pool_product(3)
            phase(N_OUT0 // 2, A_hi, A_lo, a_ready, 0)

            def mlp(v, n0, fill):
                mean_of_squares(v)
                with pe.Fori(0, FB) as fb:
                    phase(n0 // 2 + fb * KT, G_hi, G_lo, g_ready, KT * v)
                    phase((n0 + KT) // 2 + fb * KT, A_hi, A_lo, a_ready, KT * fill + fb * KT)

            mlp(1, N_MLP0, 1)

            def scores(g, tile):
                t, a = tile // 2, tile % 2
                w = min(BAND, P * (t + 1))
                banks = 2 if w > HALF else 1
                n = w // banks
                own = slice(DH * a, DH * (a + 1))
                first = tile % 2 if banks == 1 else 0
                read = tile - 1 if banks == 1 else tile
                if read > 0:
                    pe.wait_ge(negm_ready, g * (2 * QT) + read)
                queries = slice(P * t, P * (t + 1))
                for c in range(banks):
                    keys = slice(P * (t + 1) - w + n * c, P * (t + 1) - w + n * (c + 1))
                    pe.matmul(PM[:, first + c, 0:n], Q_s[a][:, queries], K_s[a][:, keys], start=True, stop=False)
                for c in range(banks):
                    keys = slice(P * (t + 1) - w + n * c, P * (t + 1) - w + n * (c + 1))
                    last = pe.matmul(PM[:, first + c, 0:n], Q_s[a][own, queries], K_lo[own, keys],
                                     start=False, stop=True)
                last.then_inc(s_done, 1)

            def first_scores(g):
                pe.wait_ge(qk_ready, 2 * g + 2)
                if not isinstance(g, int) or g:
                    pe.wait_ge(a_ready, KT * (FB + 1) + g)
                scores(g, 0)
                scores(g, 1)

            def attend(g, tile):
                t, a = tile // 2, tile % 2
                w = min(BAND, P * (t + 1))
                pe.wait_ge(pt_ready, g * (2 * QT) + (tile + 1))
                if tile >= 2:
                    pe.wait_ge(o_free, g * (2 * QT) + (tile - 1))
                for b in range(w // P):
                    for part in (0, 1):
                        last = pe.matmul(O_ps[a], PT[:, a, part, P * b:P * (b + 1)],
                                         VV[:, t + 1 - w // P + b, :],
                                         start=(b == 0 and part == 0), stop=(b == w // P - 1 and part == 1))
                last.then_inc(o_done, 1)

            def attention(g, n):
                pe.wait_ge(unit_read, n)
                for c in range(QT):
                    last = pe.transpose(PMf[:, S + P * c:S + P * (c + 1)], v_in[:, P * c:P * (c + 1)],
                                        ident)
                last.then_inc(av_turned, 1)
                for tile in range(2 * QT):
                    t, a = tile // 2, tile % 2
                    w = min(BAND, P * (t + 1))
                    pe.wait_ge(exp_done, g * (2 * QT) + (tile + 1))
                    if tile >= 2:
                        pe.wait_ge(pt_ready, g * (2 * QT) + (tile - 1))
                    for b in range(w // P):
                        last = pe.transpose(turned[a][:, P * b:P * (b + 1)], prob[a][:, P * b:P * (b + 1)], ident)
                    last.then_inc(pt_done, 1)
                    if tile + 2 < 2 * QT:
                        scores(g, tile + 2)
                    if tile == 1:
                        pe.wait_ge(av_ready, g + 1)
                    if tile:
                        attend(g, tile - 1)
                attend(g, 2 * QT - 1)

            def turn_output(g):
                pe.wait_ge(o_free, g * (2 * QT) + 2 * QT)
                for t in range(QT):
                    last = pe.transpose(PMf[:, P * t:P * (t + 1)], O_sb[:, t, :], ident)
                last.then_inc(ot_done, 1)

            def pair_units(g, j, slot):
                for u in range(3):
                    n = slot + u
                    unit(j + n // 2, n % 2, G_hi, G_lo, between=(lambda: first_scores(g)) if u == 2 else None)
                    if u == 0:
                        turn_output(g - 1)

            mean_of_squares(2)
            j = N_ATT // 2
            unit(j, 0, G_hi, G_lo, g_ready, 2 * KT)
            unit(j, 1, G_hi, G_lo)
            unit(j + 1, 0, G_hi, G_lo, between=lambda: first_scores(0))
            attention(0, N_ATT + 3)
            with pe.Fori(0, ATT_GROUPS // 2 - 1) as i:
                for b in (1, 2):
                    pair_units(2 * i + b, j + 3 * i + 3 * b // 2, 3 * b % 2)
                    attention(2 * i + b, N_ATT + 3 * b + 3 + 6 * i)
            g = ATT_GROUPS - 1
            pair_units(g, j + 3 * g // 2, 3 * g % 2)
            attention(g, N_ATT + 3 * g + 3)
            turn_output(g)
            phase(N_OUT1 // 2, A_hi, A_lo, a_ready, KT * (FB + 1))
            mlp(3, N_MLP1, FB + 2)
            mean_of_squares(4)

        @block.scalar
        def _(act):
            chain = Chain(act, act_step)

            def split_w(j, s):
                if isinstance(j, int) and 2 * j + s >= N_UNITS:
                    return
                act.wait_ge(raw_landed[s], 16 * j + 16)
                if not (isinstance(j, int) and j == 0):
                    act.wait_ge(unit_done, 2 * j + s - 1)
                act.copy(W_hi[:, s, :, :].rearrange("p k n -> p (k n)"), raw[:, s, :]).then_inc(w_hi, 1)

            def split_g(v, m):
                act.wait_ge(g_src, KT * v + m + 1)
                act.copy(G_hi[:, m, :], T[:, m % 2, :]).then_inc(g_hi, 1)

            def square_x(v, m):
                if m >= 2:
                    act.wait_ge(ss_added, KT * v + m - 1)
                act.activation(T[:, 2 + m % 2, :], X[:, m, :], ACT.Square).then_inc(sq_ready, 1)

            def root(v):
                act.wait_ge(stat_done, v + 1)
                act.activation(R[:, :], PMf[:, 0:S], ACT.Sqrt, bias=eps[:, 0:1]).then_inc(sd_ready, 1)

            def split_a(at, src, m):
                act.wait_ge(a_src, at + 1)
                act.copy(A_hi[:, m, :], src).then_inc(a_hi, 1)

            split_w(0, 0)
            for m in range(KT):
                split_g(0, m)
                if m == 1:
                    split_w(0, 1)
            act.wait_ge(const_set, 1)
            for m in range(KT):
                square_x(0, m)
            root(0)

            def gn_square(h):
                act.wait_ge(gn_centered, h + 1)
                act.activation(sq_head, OT, ACT.Square).then_inc(gn_sq, 1)

            def gn_root(h):
                act.wait_ge(gn_var, h + 1)
                act.activation(T[:, 3, :], PMf[:, S:2 * S], ACT.Sqrt, bias=eps[:, 1:2]).then_inc(gn_sd, 1)
                act.wait_ge(a_src, h + 1)
                act.copy(A_hi[:, bass.ds(h, 1), :], T[:, 3:4, :]).then_inc(a_hi, 1)

            def head(h, first):
                split_w(2 * h + 1, 0)
                if not first:
                    gn_square(h - 1)
                split_w(2 * h + 1, 1)
                if not first:
                    gn_root(h - 1)
                split_w(2 * h + 2, 0)
                split_w(2 * h + 2, 1)
                act.wait_ge(v_turned, h + 1)
                act.copy(V, PMf[:, 0:S]).then_inc(v_ready, 1)
                act.wait_ge(unit_read, 4 * h + 4)
                act.activation(T[:, 3, :], gate, ACT.Exp, scale=-1.0).then_inc(gate_exp, 1)
                for half in (0, 1):
                    act.wait_ge(pv_done, h * N_RET + (4 if half == 0 else N_RET))
                    act.copy(OT[:, HALF * half:HALF * (half + 1)], PM[:, 3, :]).then_inc(o_evac, 1)

            head(0, True)
            with act.Fori(1, RET_HEADS) as h:
                head(h, False)
            j = 2 * RET_HEADS
            split_w(j + 1, 0)
            gn_square(RET_HEADS - 1)
            split_w(j + 1, 1)
            gn_root(RET_HEADS - 1)
            for i in range(POOL_GROUPS):
                if i < 2:
                    split_w(j + 2, i)
                split_a(RET_HEADS + i, T[:, 2, :], RET_HEADS + i)

            def finish_norm(v, j0):
                for m in range(KT):
                    split_w(j0 + 1 + m // 2, m % 2)
                    if v < 4:
                        split_g(v, m)
                    else:
                        act.wait_ge(unit_read, 2 * j0 + m + 1)
                    square_x(v, m)
                root(v)

            def mlp_in(n0, fill, fb):
                per = 2
                with act.Fori(0, KT // 2) as i:
                    outer = chain.enter(i, per)
                    for s in (0, 1):
                        act.wait_ge(unit_read, n0 + fb * (2 * KT) + 2 * i + (s + 1))
                        chain.link(act.activation(T[:, 2 + s, :], T[:, s, :], ACT.Square))
                        act.copy(A_hi[:, bass.ds(2 * i + s, 1), :], T[:, 2 + s:3 + s, :]).then_inc(a_hi, 1)
                        split_w(n0 // 2 + fb * KT + i + 1, s)
                    chain.leave(outer, per, KT // 2)

            def mlp(v, n0, fill):
                per = KT
                with act.Fori(0, FB - 1) as fb:
                    outer = chain.enter(fb, per)
                    mlp_in(n0, fill, fb)
                    with act.Fori(0, KT // 2) as i:
                        for s in (0, 1):
                            split_w((n0 + KT) // 2 + fb * KT + i + 1, s)
                    chain.leave(outer, per, FB - 1)
                mlp_in(n0, fill, FB - 1)
                finish_norm(v, (n0 + KT) // 2 + (FB - 1) * KT)

            finish_norm(1, N_OUT0 // 2)
            mlp(2, N_MLP0, 1)

            def exp_tile(g, tile):
                a, w = tile % 2, min(BAND, P * (tile // 2 + 1))
                act.wait_ge(negm_ready, g * (2 * QT) + (tile + 1))
                act.activation(prob[a][:, 0:w], prob[a][:, 0:w], ACT.Exp, scale=-1.0,
                               bias=row[:, 16 + tile:17 + tile], accum_out=row[:, 32 + tile:33 + tile]).then_inc(exp_done, 1)

            def attention(g):
                act.wait_ge(av_turned, g + 1)
                act.copy(VV[:, :, 0:P], PMf[:, S:2 * S].rearrange("p (k n) -> p k n", k=QT)).then_inc(av_hi, 1)
                for tile in range(2 * QT):
                    a, w = tile % 2, min(BAND, P * (tile // 2 + 1))
                    act.wait_ge(pt_done, g * (2 * QT) + (tile + 1))
                    act.copy(PT[:, a, 0, 0:w], turned[a][:, 0:w]).then_inc(pt_hi, 1)
                    if tile + 2 < 2 * QT:
                        exp_tile(g, tile + 2)

            def hi_parts(u, g, n):
                act.wait_ge(unit_read, n)
                src, to = (q_in, Q_s) if u == 0 else (k_in, K_s)
                for a in (0, 1):
                    own = slice(DH * a, DH * (a + 1))
                    act.copy(to[a][own, :], src[own, :]).then_inc(qk_hi, 1)

            def output_hi(g):
                act.wait_ge(ot_done, g + 1)
                act.copy(A_hi[:, bass.ds(g, 1), :] if not isinstance(g, int) else A_hi[:, g, :],
                         PMf[:, 0:S] if isinstance(g, int) else
                         PMf[:, 0:S].rearrange("p (o n) -> p o n", o=1)).then_inc(a_hi, 1)

            def pair(g, j, slot, n):
                hi_parts(0, g, n + 1)
                split_w(j + (slot + 2) // 2, slot)
                if not isinstance(g, int) or g:
                    output_hi(g - 1)
                hi_parts(1, g, n + 2)
                split_w(j + (slot + 3) // 2, 1 - slot)
                exp_tile(g, 0)
                exp_tile(g, 1)
                split_w(j + (slot + 4) // 2, slot)
                attention(g)

            j = N_ATT // 2
            pair(0, j, 0, N_ATT)
            with act.Fori(0, ATT_GROUPS // 2 - 1) as i:
                for b in (1, 2):
                    pair(2 * i + b, j + 3 * i + 3 * b // 2, 3 * b % 2, N_ATT + 3 * b + 6 * i)
            g = ATT_GROUPS - 1
            pair(g, j + 3 * g // 2, 3 * g % 2, N_ATT + 3 * g)
            output_hi(g)
            finish_norm(3, N_OUT1 // 2)
            mlp(4, N_MLP1, FB + 2)

        @block.vector
        def _(dve):
            chain = Chain(dve, dve_step)
            link = chain.link

            def banks(s):
                return PUf[:, S * s:S * (s + 1)]

            def split_w(j, s):
                if isinstance(j, int) and 2 * j + s >= N_UNITS:
                    return
                dve.wait_ge(w_hi, 2 * j + s + 1)
                dve.tensor_tensor(W_lo[:, s, :, :].rearrange("p k n -> p (k n)"), raw[:, s, :],
                                  W_hi[:, s, :, :].rearrange("p k n -> p (k n)").bitcast(F32),
                                  ALU.subtract).then_inc(w_lo, 1)

            def scale_g(v, m):
                at = C_GAIN + KT * v + m
                if m >= 2:
                    dve.wait_ge(g_ready, KT * v + m - 1)
                dve.tensor_scalar(T[:, m % 2, :], X[:, m, :], C[:, at:at + 1], None, ALU.mult).then_inc(g_src, 1)

            def split_g(v, m):
                dve.wait_ge(g_hi, KT * v + m + 1)
                dve.tensor_tensor(G_lo[:, m, :], T[:, m % 2, :], G_hi[:, m, :].bitcast(F32),
                                  ALU.subtract).then_inc(g_ready, 1)

            def add_squares(v, m):
                dve.wait_ge(sq_ready, KT * v + m + 1)
                if m == 0:
                    dve.tensor_copy(R[:, :], T[:, 2, :]).then_inc(ss_added, 1)
                else:
                    dve.wait_ge(ss_added, KT * v + m)
                    dve.tensor_tensor(R[:, :], R[:, :], T[:, 2 + m % 2, :], ALU.add).then_inc(ss_added, 1)

            def inverse_root(v):
                dve.wait_ge(sd_ready, v + 1)
                dve.reciprocal(R[:, :], R[:, :]).then_inc(r_ready, 1)
                dve.wait_ge(r_ready, v + 1)

            def done(j, s):
                dve.wait_ge(unit_done, 2 * j + s + 1)

            dve.memset(ones_d[:, :], 1.0 / D)
            dve.memset(ones_h[:, :], 1.0 / P)
            dve.memset(row[:, 94:95], 0.0)
            dve.memset(eps[:, 0:1], RMS_EPS)
            dve.memset(eps[:, 1:2], GN_EPS).then_inc(const_set, 1)
            dve.wait_ge(const_landed, 16)
            split_w(0, 0)
            for m in range(KT + 1):
                if m < KT:
                    dve.wait_ge(x_landed[m], 16)
                    scale_g(0, m)
                if m >= 1:
                    split_g(0, m - 1)
                if m == 2:
                    split_w(0, 1)
            for m in range(KT):
                add_squares(0, m)
            inverse_root(0)
            dve.wait_ge(rot_landed, 16)
            link(dve.tensor_tensor(cosR, cosR, R[:, :], ALU.mult))
            link(dve.tensor_tensor(sinR, sinR, R[:, :], ALU.mult))

            def rotate(j, s, dst):
                done(j, s)
                if not (isinstance(j, int) and j + s == 0):
                    dve.wait_ge(rotated, j + s)
                dve.tensor_tensor(dst, banks(s), cosR, ALU.mult)
                dve.tensor_tensor(T[0:64, 2, :], banks(s)[64:128], sinR[0:64], ALU.mult)
                ins = dve.tensor_tensor(T[64:128, 2, :], banks(s)[0:64], sinR[64:128], ALU.mult)
                ins.then_inc(unit_read, 1)
                dve.wait_ge(unit_read, 2 * j + s + 1)
                dve.tensor_tensor(dst, dst, T[:, 2, :], ALU.add).then_inc(rotated, 1)

            def gn_center(h):
                dve.wait_ge(gn_mean, h + 1)
                dve.tensor_tensor(OT, OT, PMf[:, 0:S], ALU.subtract).then_inc(gn_centered, 1)

            def gn_scale(h):
                dve.wait_ge(gn_sd, h + 1)
                link(dve.reciprocal(T[:, 3, :], T[:, 3, :]))
                link(dve.tensor_tensor(T[:, 3, :], T[:, 3, :], OT, ALU.mult))
                gain = C[:, C_GN + h:C_GN + h + 1] if isinstance(h, int) else C[:, bass.ds(h + C_GN, 1)]
                dve.scalar_tensor_tensor(out=T[:, 3, :], in0=T[:, 3, :], scalar=gain, in1=gate, op0=ALU.mult,
                                         op1=ALU.mult).then_inc(a_src, 1)
                dve.wait_ge(a_hi, h + 1)
                dve.tensor_tensor(A_lo[:, bass.ds(h, 1), :], T[:, 3:4, :], A_hi[:, bass.ds(h, 1), :].bitcast(F32),
                                  ALU.subtract).then_inc(a_ready, 1)

            def head(h, first):
                rotate(2 * h, 0, qT)
                split_w(2 * h + 1, 0)
                if not first:
                    gn_center(h - 1)
                rotate(2 * h, 1, kT)
                split_w(2 * h + 1, 1)
                if not first:
                    gn_scale(h - 1)
                done(2 * h + 1, 0)
                dve.tensor_tensor(vT, banks(0), R[:, :], ALU.mult).then_inc(unit_read, 1)
                split_w(2 * h + 2, 0)
                done(2 * h + 1, 1)
                dve.tensor_tensor(gate, banks(1), R[:, :], ALU.mult).then_inc(unit_read, 1)
                split_w(2 * h + 2, 1)
                dve.wait_ge(dec_landed, 16 * h + 16)
                for x, (q0, n, kt) in enumerate(RET_STEPS):
                    dve.wait_ge(score_done, h * N_RET + (x + 1))
                    if x >= 3:
                        dve.wait_ge(pv_done, h * N_RET + (x - 2))
                    dve.tensor_tensor(probs[x % 3][:, 0:n], PM[:, x % 3, 0:n],
                                      dec[:, q0 - P * kt:q0 - P * kt + n], ALU.mult).then_inc(p_ready, 1)
                dve.wait_ge(gate_exp, h + 1)
                link(dve.tensor_scalar(T[:, 3, :], T[:, 3, :], 1.0, None, ALU.add))
                link(dve.reciprocal(T[:, 3, :], T[:, 3, :]))
                link(dve.tensor_tensor(gate, gate, T[:, 3, :], ALU.mult))

            head(0, True)
            with dve.Fori(1, RET_HEADS) as h:
                outer = chain.enter(h - 1, 5)
                head(h, False)
                chain.leave(outer, 5, RET_HEADS - 1)

            def pool_window(j, s, i):
                done(j, s)
                if i:
                    dve.wait_ge(pooled, i)
                tok = X[:, 0, :]
                ins = dve.tensor_tensor(tok, banks(s), R[:, :], ALU.mult)
                ins.then_inc(unit_read, 1)
                dve.wait_ge(unit_read, 2 * j + s + 1)
                cur = tok
                for step in range(i + 1):
                    lag = 1 << step
                    nxt = X[:, 1 if step % 2 == 0 else 3, :]
                    dve.tensor_copy(nxt[:, 0:lag], cur[:, 0:lag])
                    link(dve.tensor_tensor(nxt[:, lag:S], cur[:, lag:S], cur[:, 0:S - lag], ALU.add))
                    cur = nxt
                y = X[:, 6 + i % 2, :]
                cnt = C[:, C_CNT + EDGE * i:C_CNT + EDGE * (i + 1)]
                link(dve.tensor_tensor(y[:, 0:EDGE], cur[:, 0:EDGE], cnt, ALU.mult))
                dve.tensor_tensor(y[:, 0:EDGE], y[:, 0:EDGE], tok[:, 0:EDGE], ALU.subtract)
                dve.scalar_tensor_tensor(out=y[:, EDGE:S], in0=cur[:, EDGE:S], scalar=1.0 / POOL_WINDOWS[i],
                                         in1=tok[:, EDGE:S], op0=ALU.mult, op1=ALU.subtract).then_inc(pooled, 1)

            def pool_scale(i):
                dve.wait_ge(pool_mm, i + 1)
                dve.wait_ge(a_ready, RET_HEADS + i)
                dve.tensor_scalar(T[:, 2, :], PMf[:, S * (i % 2):S * (i % 2 + 1)], C[:, C_PS + i:C_PS + i + 1],
                                  None, ALU.mult).then_inc(a_src, 1)
                at = RET_HEADS + i
                dve.wait_ge(a_hi, at + 1)
                dve.tensor_tensor(A_lo[:, at, :], T[:, 2, :], A_hi[:, at, :].bitcast(F32),
                                  ALU.subtract).then_inc(a_ready, 1)

            j = 2 * RET_HEADS
            pool_window(j, 0, 0)
            split_w(j + 1, 0)
            gn_center(RET_HEADS - 1)
            pool_window(j, 1, 1)
            split_w(j + 1, 1)
            gn_scale(RET_HEADS - 1)
            pool_window(j + 1, 0, 2)
            split_w(j + 2, 0)
            pool_scale(0)
            pool_window(j + 1, 1, 3)
            split_w(j + 2, 1)
            pool_scale(1)
            pool_scale(2)
            pool_scale(3)

            def add_unit(j, s, m):
                done(j, s)
                x = X[:, m, :] if isinstance(m, int) else X[:, bass.ds(m, 1), :]
                src = banks(s) if isinstance(m, int) else banks(s).rearrange("p (o n) -> p o n", o=1)
                return dve.tensor_tensor(x, x, src, ALU.add)

            def finish_norm(v, j0, landed=0):
                for m in range(KT):
                    if landed:
                        dve.wait_ge(x_landed[m], landed)
                    add_unit(j0 + m // 2, m % 2, m).then_inc(unit_read, 1)
                    dve.wait_ge(unit_read, 2 * j0 + m + 1)
                    if v < 4:
                        scale_g(v, m)
                        split_g(v, m)
                    split_w(j0 + 1 + m // 2, m % 2)
                    add_squares(v, m)
                inverse_root(v)

            def mlp_in(n0, fill, fb):
                with dve.Fori(0, KT // 2) as i:
                    for s in (0, 1):
                        j = n0 // 2 + fb * KT + i
                        at = KT * fill + fb * KT + 2 * i + s
                        done(j, s)
                        dve.scalar_tensor_tensor(out=T[:, s, :], in0=banks(s), scalar=0.0, in1=R[:, :], op0=ALU.max,
                                                 op1=ALU.mult).then_inc(unit_read, 1)
                        dve.wait_ge(a_hi, at + 1)
                        dve.tensor_tensor(A_lo[:, bass.ds(2 * i + s, 1), :], T[:, 2 + s:3 + s, :],
                                          A_hi[:, bass.ds(2 * i + s, 1), :].bitcast(F32),
                                          ALU.subtract).then_inc(a_ready, 1)
                        split_w(j + 1, s)

            def mlp(v, n0, fill):
                with dve.Fori(0, FB - 1) as fb:
                    mlp_in(n0, fill, fb)
                    with dve.Fori(0, KT // 2) as i:
                        for s in (0, 1):
                            j = (n0 + KT) // 2 + fb * KT + i
                            add_unit(j, s, 2 * i + s).then_inc(unit_read, 1)
                            split_w(j + 1, s)
                mlp_in(n0, fill, FB - 1)
                finish_norm(v, (n0 + KT) // 2 + (FB - 1) * KT)

            finish_norm(1, N_OUT0 // 2, landed=32)
            mlp(2, N_MLP0, 1)
            dve.wait_ge(spilled, 16 * KT)

            def output(g, tile, part):
                t, a = tile // 2, tile % 2
                to, share = O_sb[:, t, DH * a:DH * (a + 1)], row[:, 48 + tile:49 + tile]
                of = O_ps[a][:, P * part + DH * a:P * part + DH * (a + 1)]
                if part == 0:
                    dve.wait_ge(share_ready, g * (2 * QT) + (tile + 1))
                    dve.wait_ge(o_done, g * (2 * QT) + (tile + 1))
                    link(dve.tensor_scalar(to, of, share, None, ALU.mult))
                else:
                    dve.scalar_tensor_tensor(out=to, in0=of, scalar=share, in1=to, op0=ALU.mult,
                                             op1=ALU.add).then_inc(o_free, 1)

            def biased(g, tile):
                a, w = tile % 2, min(BAND, P * (tile // 2 + 1))
                banks = 2 if w > HALF else 1
                first = tile % 2 if banks == 1 else 0
                dve.wait_ge(s_done, g * (2 * QT) + (tile + 1))
                dve.memset(row[:, 64 + tile:65 + tile], 0.0)
                two = [x.rearrange("p (c n) -> p c n", c=banks) for x in (prob[a][:, 0:w], bias[a][:, BAND - w:BAND])]
                dve.tensor_tensor_reduce(two[0], PM[:, first:first + banks, 0:w // banks], two[1], -1.0,
                                         3.0e38, ALU.add, ALU.min, row[:, 16 + tile:17 + tile]).then_inc(negm_ready, 1)

            def attention(g):
                dve.wait_ge(av_hi, g + 1)
                dve.tensor_tensor(VV[:, :, P:2 * P], PMf[:, S:2 * S].rearrange("p (k n) -> p k n", k=QT),
                                  VV[:, :, 0:P].bitcast(F32), ALU.subtract).then_inc(av_ready, 1)
                for tile in range(2 * QT):
                    a, w = tile % 2, min(BAND, P * (tile // 2 + 1))
                    if tile + 2 < 2 * QT:
                        biased(g, tile + 2)
                    dve.wait_ge(pt_hi, g * (2 * QT) + (tile + 1))
                    dve.reciprocal(row[:, 48 + tile:49 + tile], row[:, 32 + tile:33 + tile]).then_inc(share_ready, 1)
                    dve.tensor_tensor(PT[:, a, 1, 0:w], turned[a][:, 0:w], PT[:, a, 0, 0:w].bitcast(F32),
                                      ALU.subtract).then_inc(pt_ready, 1)
                    if tile:
                        output(g, tile - 1, 0)
                        output(g, tile - 1, 1)
                output(g, 2 * QT - 1, 0)
                output(g, 2 * QT - 1, 1)

            def output_lo(g):
                dve.wait_ge(a_hi, KT * (FB + 1) + g + 1)
                dve.tensor_tensor(A_lo[:, bass.ds(g, 1), :], PMf[:, 0:S].rearrange("p (o n) -> p o n", o=1),
                                  A_hi[:, bass.ds(g, 1), :].bitcast(F32), ALU.subtract).then_inc(a_ready, 1)

            def pair(g, j, slot):
                def at(u):
                    return j + (slot + u) // 2, (slot + u) % 2

                done(*at(0))
                dve.scalar_tensor_tensor(out=q_in, in0=banks(at(0)[1]), scalar=DH ** -0.5, in1=R[:, :],
                                         op0=ALU.mult, op1=ALU.mult).then_inc(unit_read, 1)
                dve.wait_ge(qk_hi, 4 * g + 2)
                for a in (0, 1):
                    own, other = slice(DH * a, DH * (a + 1)), slice(DH * (1 - a), DH * (2 - a))
                    ins = dve.tensor_tensor(Q_s[a][other, :], q_in[own, :], Q_s[a][own, :].bitcast(F32), ALU.subtract)
                ins.then_inc(qk_ready, 1)
                split_w(j + (slot + 2) // 2, slot)
                if not isinstance(g, int) or g:
                    output_lo(g - 1)
                done(*at(1))
                dve.tensor_tensor(k_in, banks(at(1)[1]), R[:, :], ALU.mult).then_inc(unit_read, 1)
                dve.wait_ge(unit_read, 2 * at(1)[0] + (at(1)[1] + 1))
                for a in (0, 1):
                    own, other = slice(DH * a, DH * (a + 1)), slice(DH * (1 - a), DH * (2 - a))
                    dve.tensor_copy(K_s[a][other, :], k_in[own, :])
                dve.wait_ge(qk_hi, 4 * g + 4)
                for a in (0, 1):
                    own = slice(DH * a, DH * (a + 1))
                    ins = dve.tensor_tensor(K_lo[own, :], k_in[own, :], K_s[a][own, :].bitcast(F32), ALU.subtract)
                ins.then_inc(qk_ready, 1)
                split_w(j + (slot + 3) // 2, 1 - slot)
                if isinstance(g, int) and g == 0:
                    dve.wait_ge(b_masked, 4)
                dve.wait_ge(b_ready, g * 8 + 8)
                biased(g, 0)
                biased(g, 1)
                done(*at(2))
                dve.tensor_tensor(v_in, banks(at(2)[1]), R[:, :], ALU.mult).then_inc(unit_read, 1)
                split_w(j + (slot + 4) // 2, slot)
                attention(g)

            j = N_ATT // 2
            per = 2 * QT
            pair(0, j, 0)
            with dve.Fori(0, ATT_GROUPS // 2 - 1) as i:
                outer = chain.enter(i, 2 * per)
                for b in (1, 2):
                    pair(2 * i + b, j + 3 * i + 3 * b // 2, 3 * b % 2)
                chain.leave(outer, 2 * per, ATT_GROUPS // 2 - 1)
            g = ATT_GROUPS - 1
            pair(g, j + 3 * g // 2, 3 * g % 2)
            output_lo(g)
            finish_norm(3, N_OUT1 // 2, landed=48)
            mlp(4, N_MLP1, FB + 2)
            for m in range(KT):
                at = C_GAIN + KT * 4 + m
                dve.scalar_tensor_tensor(out=X[:, m, :], in0=X[:, m, :], scalar=C[:, at:at + 1], in1=R[:, :],
                                         op0=ALU.mult, op1=ALU.mult).then_inc(y_ready, 1)


def _units(w):
    rows, cols = w.shape[0] // D, w.shape[1] // P
    return w.reshape(rows, KT, P, cols, P).transpose(0, 3, 2, 1, 4).reshape(rows * cols, P, D)


def _tables():
    import numpy as np
    f = np.float32
    half = P // 2
    inv_freq = f(1.0) / np.power(f(10000.0), np.linspace(0.0, 1.0, half, dtype=f), dtype=f)
    ang = (np.arange(S, dtype=f)[:, None] * inv_freq[None, :]).astype(f).T
    cos, sin = np.cos(ang.astype(np.float64)), np.sin(ang.astype(np.float64))
    rot = np.stack([np.concatenate([cos, cos]), np.concatenate([-sin, sin])], 1).astype(f)
    p, c = np.arange(P)[:, None], np.arange(S)[None, :]
    log_g = np.log1p(-np.exp2(-5.0 - np.arange(RET_HEADS)))
    decay = np.exp(np.abs(c - p)[None] * log_g[:, None, None])
    decay = np.where(c // DH < p // DH, 0.0, decay) * P ** -0.5
    tokens = np.arange(EDGE) + 1
    cnt = np.concatenate([1.0 / np.minimum(tokens, w) for w in POOL_WINDOWS])
    return rot, decay.astype(f), cnt.astype(f)


def kernel(x, mix_norm, ffn_norm, w_ffn_in, w_ffn_out, ab_w_in, ab_gn_gain, ab_w_pool, ab_pool_scale, ab_w_out,
           c_w_qkv, c_rel_bias, c_w_out, final_norm):
    import numpy as np
    import concourse.bacc as bacc
    from concourse.bass_utils import run_bass_kernel_spmd

    (x, mix_norm, ffn_norm, w_ffn_in, w_ffn_out, ab_w_in, ab_gn_gain, ab_w_pool, ab_pool_scale, ab_w_out, c_w_qkv,
     c_rel_bias, c_w_out, final_norm) = map(np.asarray, (
         x, mix_norm, ffn_norm, w_ffn_in, w_ffn_out, ab_w_in, ab_gn_gain, ab_w_pool, ab_pool_scale, ab_w_out, c_w_qkv,
         c_rel_bias, c_w_out, final_norm))

    ret = RET_HEADS * P
    w_in = ab_w_in[0]
    turned = np.concatenate([np.arange(0, P, 2), np.arange(1, P, 2)])
    parts = []
    for h in range(RET_HEADS):
        for part in range(4):
            w = w_in[:, part * ret + h * P:part * ret + (h + 1) * P]
            parts.append(_units(w[:, turned] if part < 2 else w))
    parts += [_units(w_in[:, 4 * ret:]), _units(ab_w_out[0])]

    def mlp(layer):
        for fb in range(FB):
            parts.append(_units(w_ffn_in[layer][:, fb * D:(fb + 1) * D]))
            parts.append(_units(w_ffn_out[layer][fb * D:(fb + 1) * D]))

    mlp(0)
    for g in range(ATT_GROUPS):
        parts.extend(_units(c_w_qkv[0][:, part * D + g * P:part * D + (g + 1) * P]) for part in range(3))
    parts.append(_units(c_w_out[0]))
    mlp(1)
    weights = np.concatenate(parts)

    rot, decay, cnt = _tables()
    norms = [mix_norm[0], ffn_norm[0], mix_norm[1], ffn_norm[1], final_norm]
    small = np.concatenate(
        [np.eye(P, dtype=np.float32)] + [g.reshape(KT, P).T for g in norms]
        + [ab_gn_gain[0].reshape(RET_HEADS, P).T, ab_pool_scale[0].reshape(POOL_GROUPS, P).T,
           np.broadcast_to(cnt, (P, cnt.size))], axis=1)
    n_rel = c_rel_bias.shape[-1]
    rel = c_rel_bias[0][:, np.minimum(1 + np.arange(REL_ROW), n_rel - 1)]
    arrays = {
        "weights": weights,
        "x_in": x[0].T.reshape(KT, P, S),
        "small": small,
        "rot": rot,
        "decay": decay,
        "w_pool": ab_w_pool[0].transpose(1, 0, 2).reshape(P, POOL_GROUPS * P),
        "rel": rel,
    }
    arrays = {name: np.ascontiguousarray(a) for name, a in arrays.items()}
    nc = bacc.Bacc("TRN2", target_bir_lowering=False, num_devices=1)
    args = [nc.dram_tensor(name, a.shape, F32, kind="ExternalInput").ap() for name, a in arrays.items()]
    out = nc.dram_tensor("out", (KT, P, S), F32, kind="ExternalOutput").ap()
    spill = nc.dram_tensor("spill", (KT, P, S), F32).ap()
    trunk_kernel(nc, *args, out, spill)
    result = run_bass_kernel_spmd(nc, [arrays], core_ids=[0]).results[0]["out"]
    return np.ascontiguousarray(result.reshape(D, S).T)[None]
```

```python
from contextlib import ExitStack

import concourse.bass as bass
from concourse import mybir

P = 128
D = 1024
S = 1024
KT = D // P
HALF = 512
FB = 4
RET_HEADS = 4
POOL_WINDOWS = (2, 4, 8, 16)
POOL_GROUPS = len(POOL_WINDOWS)
EDGE = POOL_WINDOWS[-1]
ATT_GROUPS = 8
DH = 64
QT = S // P
BAND = 640
REL = 256
REL_ROW = 383
RMS_EPS = 1e-6
GN_EPS = 1e-5
MASKED = -1e30

N_OUT0 = 4 * RET_HEADS + POOL_GROUPS
N_MLP0 = N_OUT0 + KT
N_ATT = N_MLP0 + 2 * KT * FB
N_OUT1 = N_ATT + 3 * ATT_GROUPS
N_MLP1 = N_OUT1 + KT
N_UNITS = N_MLP1 + 2 * KT * FB


def head_pair(h):
    return 0 if isinstance(h, int) and h == 0 else 2 * h + POOL_GROUPS // 2


def head_tile(h):
    return 0 if isinstance(h, int) and h == 0 else h + POOL_GROUPS


EARLY = 3


def squares(v, m):
    return KT * v + m + 1 - EARLY


HT = HALF // P
RET_STEPS = [(P * j, HALF * (half + 1) - P * j, j) for half in (0, 1) for j in range(HT * half, HT * (half + 1))]
N_RET = len(RET_STEPS)

C_ID = 0
C_GAIN = C_ID + P
C_GN = C_GAIN + 5 * KT
C_PS = C_GN + RET_HEADS
C_CNT = C_PS + POOL_GROUPS
C_ALL = C_CNT + POOL_GROUPS * EDGE

F32 = mybir.dt.float32
F32R = mybir.dt.float32r
ALU = mybir.AluOpType
ACT = mybir.ActivationFunctionType


class Chain:

    def __init__(self, eng, sem):
        self.eng, self.sem, self.base, self.k = eng, sem, 0, 0

    def link(self, ins):
        ins.then_inc(self.sem, 1)
        self.k += 1
        self.eng.wait_ge(self.sem, self.base + self.k)

    def enter(self, i, per):
        outer = (self.base, self.k)
        self.base, self.k = self.base + self.k + i * per, 0
        return outer

    def leave(self, outer, per, count):
        assert self.k == per, (self.k, per)
        self.base, self.k = outer[0], outer[1] + per * count


def trunk_kernel(nc, weights, x_in, small, rot, decay, key_decay, w_pool, rel, out, spill):
    with ExitStack() as ctx:
        def sb(name, shape, dt=F32):
            return ctx.enter_context(nc.sbuf_tensor(name, shape, dt))

        def sem(name):
            return ctx.enter_context(nc.semaphore(name))

        def next_place():
            return (nc.sbuf_base + 31) // 32 * 32

        x_at = next_place()
        X = sb("X", [P, KT, S])
        G_hi = sb("G_hi", [P, KT, S], F32R)
        G_lo = sb("G_lo", [P, KT, S], F32R)
        a_at = next_place()
        A_hi = sb("A_hi", [P, KT, S], F32R)
        A_lo = sb("A_lo", [P, KT, S], F32R)
        raw = sb("raw", [P, 2, S])
        W_hi = sb("W_hi", [P, 2, KT, P], F32R)
        W_lo = sb("W_lo", [P, 2, KT, P], F32R)
        R = sb("R", [P, S])
        t_at = next_place()
        T = sb("T", [P, 4, S])
        C = sb("C", [P, C_ALL])
        ones_h = sb("ones_h", [P, P])
        root = sb("root", [P, 4 * QT])
        eps = sb("eps", [P, 2])
        row = sb("row", [P, 3 * 2 * QT + 1])
        WP = sb("WP", [P, POOL_GROUPS * P])

        PU = ctx.enter_context(nc.psum_tensor("PU", [P, 4, HALF], F32))
        PM = ctx.enter_context(nc.psum_tensor("PM", [P, 4, HALF], F32))
        PUf = PU[:, :, :].rearrange("p b n -> p (b n)")
        PMf = PM[:, :, :].rearrange("p b n -> p (b n)")

        qT, kT, vT, V, gate = X[:, 0, :], X[:, 1, :], X[:, 2, :], X[:, 3, :], X[:, 4, :]
        OT = X[:, 2, :]
        Xf = X[:, :, :].rearrange("p k n -> p (k n)")
        probs = [Xf[:, 5 * S + HALF * i:5 * S + HALF * (i + 1)] for i in range(3)]
        sq_head = X[:, 5, :]
        dec = X[:, 7, :]
        cosR, sinR = T[:, 0, :], T[:, 1, :]
        O_sb = X[:, 7, :].rearrange("p (t f) -> p t f", t=QT)
        ident = C[:, C_ID:C_ID + P]

        def alias(name, shape, dt, offset):
            return nc.alloc_sbuf_tensor_at(name, shape, dt, offset=offset)

        Q_s = [alias(f"Q_s{a}", [P, S], F32R, x_at + 4 * S * a) for a in (0, 1)]
        K_s = [alias(f"K_s{a}", [P, S], F32R, x_at + 4 * S * (2 + a)) for a in (0, 1)]
        K_lo = alias("K_lo", [P, S], F32R, x_at + 4 * S * 4)
        VV = alias("VV", [P, QT, 2 * P], F32R, x_at + 4 * S * 5)
        PT = alias("PT", [P, 2, 2, BAND], F32R, t_at + 4 * 2 * BAND)
        B = [alias(f"B{a}", [P, S], F32, a_at + 4 * S * (KT * (a + 1) - 1)) for a in (0, 1)]
        bias = [B[a][:, 0:BAND] for a in (0, 1)]
        k_tok, state = B[0][:, 0:HALF], B[0][:, HALF:HALF + P]
        q_late, key_dec = B[1][:, 0:HALF], B[1][:, HALF:HALF + RET_HEADS * HT]
        rel_t = [B[a][:, BAND:BAND + REL] for a in (0, 1)]
        Tf = T[:, :, :].rearrange("p k n -> p (k n)")
        prob = [Tf[:, BAND * a:BAND * (a + 1)] for a in (0, 1)]
        turned = [[PUf[:, S * b:S * b + BAND] for b in banks] for banks in ((1, 0), (0, 1))]
        v_ps = [[PU[:, 3, :], PU[:, 1, :]], [PU[:, 1, :], PU[:, 3, :]]]
        O_ps = [PM[:, 2 + a, 0:2 * P] for a in (0, 1)]
        q_in, k_in, v_in = Tf[:, 0:S], Tf[:, 2 * BAND:2 * BAND + S], Tf[:, 2 * BAND + S:2 * BAND + 2 * S]

        raw_landed = [sem("raw_landed0"), sem("raw_landed1")]
        w_hi, w_lo = sem("w_hi"), sem("w_lo")
        unit_done = sem("unit_done")
        unit_read = sem("unit_read")
        g_hi, g_ready = sem("g_hi"), sem("g_ready")
        a_src, a_hi, a_ready = sem("a_src"), sem("a_hi"), sem("a_ready")
        sq_ready, ss_added, early_squares = sem("sq_ready"), sem("ss_added"), sem("early_squares")
        stat_done, sd_ready, inv_ready, spread_done, r_ready = (
            sem("stat_done"), sem("sd_ready"), sem("inv_ready"), sem("spread_done"), sem("r_ready"))
        x_first = [sem(f"x_first{m}") for m in range(KT)]
        x_landed = [sem(f"x_landed{m}") for m in range(KT)]
        const_landed, const_set = sem("const_landed"), sem("const_set")
        rot_landed, dec_landed, wp_landed = sem("rot_landed"), sem("dec_landed"), sem("wp_landed")
        rotated, v_turned, v_ready = sem("rotated"), sem("v_turned"), sem("v_ready")
        gate_sigmoid = sem("gate_sigmoid")
        score_done, p_ready, pv_done, o_evac = sem("score_done"), sem("p_ready"), sem("pv_done"), sem("o_evac")
        gn_mean, gn_centered, gn_sq, gn_var, gn_sd, gn_inv, gn_spread = (
            sem("gn_mean"), sem("gn_centered"), sem("gn_sq"), sem("gn_var"), sem("gn_sd"), sem("gn_inv"),
            sem("gn_spread"))
        pooled, pool_mm = sem("pooled"), sem("pool_mm")
        spilled = sem("spilled")
        qk_hi, qk_ready = sem("qk_hi"), sem("qk_ready")
        kd_landed, k_decayed, q_decayed = sem("kd_landed"), sem("k_decayed"), sem("q_decayed")
        state_done, state_ready = sem("state_done"), sem("state_ready")
        v_half_done, v_half = sem("v_half_done"), sem("v_half")
        av_turned, av_hi, av_ready = sem("av_turned"), sem("av_hi"), sem("av_ready")
        b_masked, b_landed, b_ready = sem("b_masked"), sem("b_landed"), sem("b_ready")
        s_done, negm_ready, exp_done, pt_done, pt_hi, pt_ready, o_done, o_free, ot_done = (
            sem("s_done"), sem("negm_ready"), sem("exp_done"), sem("pt_done"), sem("pt_hi"), sem("pt_ready"),
            sem("o_done"), sem("o_free"), sem("ot_done"))
        share_ready = sem("share_ready")
        y_ready, out_landed = sem("y_ready"), sem("out_landed")
        dve_step, act_step = sem("dve_step"), sem("act_step")

        block = ctx.enter_context(nc.Block())

        @block.sync
        def _(sp):
            sp.dma_start(raw[:, 0, :], weights[0]).then_inc(raw_landed[0], 16)
            for m in range(KT):
                sp.dma_start(X[:, m, :], x_in[m]).then_inc(x_first[m], 16)
                if m == 1:
                    sp.dma_start(raw[:, 1, :], weights[1]).then_inc(raw_landed[1], 16)
            with sp.Fori(1, N_UNITS // 2) as j:
                for s in (0, 1):
                    sp.wait_ge(w_lo, 2 * j + (s - 1))
                    sp.dma_start(raw[:, s:s + 1, :],
                                 weights[bass.ds(2 * j + s, 1)].rearrange("u p n -> p u n")).then_inc(raw_landed[s], 16)

        @block.gpsimd
        def _(pool):
            pool.dma_start(C[:, :], small).then_inc(const_landed, 16)
            for m in range(EARLY):
                pool.wait_ge(x_first[m], 16)
                if m >= 2:
                    pool.wait_ge(early_squares, 2 * m - 1)
                pool.tensor_tensor(B[min(m, 1)][:, :], X[:, m, :], X[:, m, :], ALU.mult).then_inc(early_squares, 1)
                if m:
                    pool.wait_ge(early_squares, 2 * m)
                    pool.tensor_tensor(B[0][:, :], B[0][:, :], B[1][:, :], ALU.add).then_inc(early_squares, 1)
            pool.dma_start(T[:, 0:2, :], rot).then_inc(rot_landed, 16)
            pool.dma_start(WP[:, :], w_pool).then_inc(wp_landed, 16)
            pool.wait_ge(r_ready, 1)
            pool.dma_start(key_dec, key_decay).then_inc(kd_landed, 16)
            pool.dma_start(dec, decay[0]).then_inc(dec_landed, 16)
            pool.wait_ge(pool_mm, POOL_GROUPS)
            with pool.Fori(1, RET_HEADS) as h:
                pool.wait_ge(p_ready, h * N_RET)
                pool.dma_start(X[:, 7:8, :], decay[bass.ds(h, 1)].rearrange("h p n -> p h n")).then_inc(dec_landed, 16)
            pool.wait_ge(pv_done, RET_HEADS * N_RET)
            for m in (0, 1, 3, 6, 7):
                pool.dma_start(X[:, m, :], x_in[m]).then_inc(x_landed[m], 16)
            pool.wait_ge(a_ready, KT)
            for m in (2, 4, 5):
                pool.dma_start(X[:, m, :], x_in[m]).then_inc(x_landed[m], 16)
            for m in range(KT):
                pool.wait_ge(unit_read, N_ATT - KT + m + 1)
                pool.dma_start(spill[m], X[:, m, :]).then_inc(spilled, 16)
            pool.wait_ge(spilled, 16 * KT)
            pool.wait_ge(r_ready, 3)
            for a in (0, 1):
                pool.memset(bias[a][0:DH, BAND - DH:BAND], MASKED).then_inc(b_masked, 1)
                pool.memset(bias[a][DH:P, 0:DH], MASKED).then_inc(b_masked, 1)

            def bias_tiles(g):
                for a in (0, 1):
                    pool.dma_start(rel_t[a], bass.AP(tensor=rel.tensor, offset=g * (2 * REL_ROW) + a * REL_ROW,
                                                     ap=[[1, P], [1, REL]])).then_inc(b_landed, 16)
                pool.wait_ge(b_landed, g * 32 + 32)
                for a in (0, 1):
                    for rows, first, end in ((slice(0, DH), 0, BAND - DH), (slice(DH, P), DH, BAND)):
                        near = rel_t[a][rows, REL - (end - (BAND - REL)):REL][:, ::-1]
                        far = rel_t[a][rows, REL - 1:REL].to_broadcast([DH, BAND - REL - first])
                        zero = row[rows, 48:49]
                        for to, of in ((slice(BAND - REL, end), near), (slice(first, BAND - REL), far)):
                            pool.tensor_tensor(bias[a][rows, to], of, zero.to_broadcast([DH, to.stop - to.start]),
                                               ALU.add).then_inc(b_ready, 1)

            bias_tiles(0)
            with pool.Fori(1, ATT_GROUPS) as g:
                pool.wait_ge(negm_ready, g * (2 * QT))
                bias_tiles(g)
            pool.wait_ge(a_ready, KT * (FB + 2))
            for m in range(KT):
                pool.dma_start(X[:, m, :], spill[m]).then_inc(x_landed[m], 16)
            for m in range(KT):
                pool.wait_ge(y_ready, m + 1)
                pool.dma_start(out[m], X[:, m, :]).then_inc(out_landed, 16)
            pool.wait_ge(out_landed, 16 * KT)

        @block.tensor
        def _(pe):
            def tiles(j, s, hi, lo, ks, ready=None, base=0):
                for k in ks:
                    if ready is not None:
                        pe.wait_ge(ready, base + k + 1)
                    for n, (w, x) in enumerate(((W_hi, hi), (W_hi, lo), (W_lo, hi))):
                        for half in (0, 1):
                            last = pe.matmul(PU[:, 2 * s + half, :], w[:, s, k, :],
                                             x[:, k, HALF * half:HALF * (half + 1)],
                                             start=(k == 0 and n == 0), stop=(k == KT - 1 and n == 2))
                return last

            def tiles_by_half(j, s, hi, lo, ks, first_done):
                for half in (0, 1):
                    for k in ks:
                        for n, (w, x) in enumerate(((W_hi, hi), (W_hi, lo), (W_lo, hi))):
                            last = pe.matmul(PU[:, 2 * s + half, :], w[:, s, k, :],
                                             x[:, k, HALF * half:HALF * (half + 1)],
                                             start=False, stop=(k == KT - 1 and n == 2))
                    if half == 0:
                        last.then_inc(first_done, 1)
                return last

            def enter_unit(j, s):
                pe.wait_ge(w_lo, 2 * j + s + 1)
                if not (isinstance(j, int) and j == 0):
                    pe.wait_ge(unit_read, 2 * j + s - 1)

            def unit(j, s, hi, lo, ready=None, base=0, between=None, tile=KT - 2,
                     first_done=None):
                enter_unit(j, s)
                if between is not None:
                    tiles(j, s, hi, lo, range(tile), ready, base)
                    between()
                if first_done is not None:
                    last = tiles_by_half(j, s, hi, lo, range(tile, KT), first_done)
                else:
                    last = tiles(j, s, hi, lo, range(tile if between is not None else 0, KT), ready, base)
                last.then_inc(unit_done, 1)

            def phase(j0, hi, lo, ready, base, norm=None, pairs=KT // 2):
                unit(j0, 0, hi, lo, ready, base, between=None if norm is None else (lambda: norm_sums(norm)),
                     tile=KT - 1)
                unit(j0, 1, hi, lo, between=None if norm is None else (lambda: spread(norm)), tile=2)
                with pe.Fori(1, pairs) as i:
                    for s in (0, 1):
                        unit(j0 + i, s, hi, lo)

            def sums(to, of):
                for c in range(QT):
                    last = pe.matmul(to[:, c:c + 1], of[:, P * c:P * (c + 1)], ones_h[:, 0:1], start=True, stop=True)
                return last

            def spread_out(to, cols):
                for c in range(QT):
                    last = pe.matmul(to[:, P * c:P * (c + 1)], root[:, cols + c:cols + c + 1].to_broadcast([P, P]),
                                     ident, start=True, stop=True)
                return last

            def norm_sums(v):
                pe.wait_ge(ss_added, squares(v, KT - 1))
                sums(PM[:, 0, :], R).then_inc(stat_done, 1)

            def spread(v):
                pe.wait_ge(inv_ready, v + 1)
                spread_out(PMf[:, 0:S], QT).then_inc(spread_done, 1)

            def group_mean(h):
                pe.wait_ge(o_evac, 2 * h + 2)
                for half in (0, 1):
                    last = pe.matmul(PM[:, half, :], ones_h[:, :], OT[:, HALF * half:HALF * (half + 1)],
                                     start=True, stop=True)
                last.then_inc(gn_mean, 1)

            def group_var(h):
                pe.wait_ge(gn_sq, h + 1)
                sums(PM[:, 2, :], sq_head).then_inc(gn_var, 1)

            def group_spread(h):
                pe.wait_ge(gn_inv, h + 1)
                spread_out(PMf[:, S:2 * S], 3 * QT).then_inc(gn_spread, 1)

            def turn_v(h):
                pe.wait_ge(unit_read, 2 * head_pair(h) + 3)
                for c in range(QT):
                    pe.transpose(PMf[:, P * c:P * (c + 1)], vT[:, P * c:P * (c + 1)], ident)
                pe.wait_ge(rotated, 2 * h + 2)
                if not (isinstance(h, int) and h == 0):
                    pe.wait_ge(a_src, h + POOL_GROUPS)
                for c in range(HT):
                    last = pe.transpose(PM[:, 2, P * c:P * (c + 1)], kT[:, P * c:P * (c + 1)], ident)
                last.then_inc(v_turned, 1)

            def retention(h):
                pe.wait_ge(v_ready, h + 1)
                pe.wait_ge(k_decayed, HT * (h + 1))
                for x in range(N_RET + 3):
                    if x == 3:
                        for c in range(HT):
                            last = pe.matmul(PU[:, 0, 0:P], k_tok[:, P * c:P * (c + 1)], V[:, P * c:P * (c + 1)],
                                             start=(c == 0), stop=(c == HT - 1))
                        last.then_inc(state_done, 1)
                    if x >= 3:
                        y = x - 3
                        q0, n, kt = RET_STEPS[y]
                        if kt == HT:
                            pe.wait_ge(o_evac, 2 * h + 1)
                            pe.wait_ge(state_ready, h + 1)
                            pe.wait_ge(q_decayed, h + 1)
                            pe.matmul(PM[:, 3, :], state, q_late, start=True, stop=False)
                        pe.wait_ge(p_ready, h * N_RET + (y + 1))
                        pe.matmul(PM[:, 3, q0 % HALF:q0 % HALF + n], V[:, P * kt:P * (kt + 1)], probs[y % 3][:, 0:n],
                                  start=(kt == 0), stop=(kt % HT == HT - 1)).then_inc(pv_done, 1)
                    if x < N_RET:
                        q0, n, kt = RET_STEPS[x]
                        pe.matmul(PM[:, x % 3, 0:n], kT[:, P * kt:P * (kt + 1)], qT[:, q0:q0 + n],
                                  start=True, stop=True).then_inc(score_done, 1)

            def pool_product(i):
                if i == 0:
                    pe.wait_ge(wp_landed, 16)
                pe.wait_ge(pooled, i + 1)
                if i >= 1:
                    pe.wait_ge(a_src, i)
                for half in (0, 1):
                    last = pe.matmul(PM[:, 2 * (i % 2) + half, :], WP[:, P * i:P * (i + 1)],
                                     X[:, 6 + i % 2, HALF * half:HALF * (half + 1)], start=True, stop=True)
                last.then_inc(pool_mm, 1)

            pe.wait_ge(const_landed, 16)
            pe.wait_ge(const_set, 1)
            unit(0, 0, G_hi, G_lo, g_ready)
            unit(0, 1, G_hi, G_lo, between=lambda: norm_sums(0))
            spread(0)
            unit(1, 0, G_hi, G_lo)
            unit(1, 1, G_hi, G_lo, between=lambda: turn_v(0))
            retention(0)
            j = head_pair(0) + 2
            unit(j, 0, G_hi, G_lo)
            group_mean(0)
            unit(j, 1, G_hi, G_lo)
            group_var(0)
            unit(j + 1, 0, G_hi, G_lo, between=lambda: group_spread(0))
            pool_product(0)
            pool_product(1)
            unit(j + 1, 1, G_hi, G_lo)
            pool_product(2)
            j = head_pair(1)
            unit(j, 0, G_hi, G_lo)
            pool_product(3)
            unit(j, 1, G_hi, G_lo)
            unit(j + 1, 0, G_hi, G_lo)
            unit(j + 1, 1, G_hi, G_lo, between=lambda: turn_v(1))
            retention(1)
            with pe.Fori(2, RET_HEADS) as h:
                j = head_pair(h)
                unit(j, 0, G_hi, G_lo)
                group_mean(h - 1)
                unit(j, 1, G_hi, G_lo)
                group_var(h - 1)
                unit(j + 1, 0, G_hi, G_lo, between=lambda: group_spread(h - 1))
                unit(j + 1, 1, G_hi, G_lo, between=lambda: turn_v(h))
                retention(h)
            j, last_head = N_OUT0 // 2, RET_HEADS - 1
            enter_unit(j, 0)
            tiles(j, 0, A_hi, A_lo, range(1), a_ready)
            group_mean(last_head)
            tiles(j, 0, A_hi, A_lo, range(1, 4), a_ready)
            group_var(last_head)
            tiles(j, 0, A_hi, A_lo, range(4, KT - 1), a_ready)
            group_spread(last_head)
            enter_unit(j, 1)
            tiles(j, 1, A_hi, A_lo, range(KT - 3))
            tiles(j, 0, A_hi, A_lo, range(KT - 1, KT), a_ready).then_inc(unit_done, 1)
            tiles(j, 1, A_hi, A_lo, range(KT - 3, KT)).then_inc(unit_done, 1)
            with pe.Fori(1, KT // 2) as i:
                for s in (0, 1):
                    unit(j + i, s, A_hi, A_lo)

            def mlp(v, n0, fill):
                phase(n0 // 2, G_hi, G_lo, g_ready, KT * v, norm=v)
                phase((n0 + KT) // 2, A_hi, A_lo, a_ready, KT * fill)
                with pe.Fori(1, FB) as fb:
                    phase(n0 // 2 + fb * KT, G_hi, G_lo, g_ready, KT * v)
                    phase((n0 + KT) // 2 + fb * KT, A_hi, A_lo, a_ready, KT * fill + fb * KT)

            mlp(1, N_MLP0, 1)

            def scores(g, tile):
                t, a = tile // 2, tile % 2
                w = min(BAND, P * (t + 1))
                banks = 2 if w > HALF else 1
                n = w // banks
                own = slice(DH * a, DH * (a + 1))
                first = tile % 2 if banks == 1 else 0
                read = tile - 1 if banks == 1 else tile
                if read > 0:
                    pe.wait_ge(negm_ready, g * (2 * QT) + read)
                queries = slice(P * t, P * (t + 1))
                for c in range(banks):
                    keys = slice(P * (t + 1) - w + n * c, P * (t + 1) - w + n * (c + 1))
                    pe.matmul(PM[:, first + c, 0:n], Q_s[a][:, queries], K_s[a][:, keys], start=True, stop=False)
                for c in range(banks):
                    keys = slice(P * (t + 1) - w + n * c, P * (t + 1) - w + n * (c + 1))
                    last = pe.matmul(PM[:, first + c, 0:n], Q_s[a][own, queries], K_lo[own, keys],
                                     start=False, stop=True)
                last.then_inc(s_done, 1)

            def first_scores(g):
                pe.wait_ge(qk_ready, 2 * g + 2)
                if not isinstance(g, int) or g:
                    pe.wait_ge(a_ready, KT * (FB + 1) + g)
                scores(g, 0)
                scores(g, 1)

            def attend(g, tile):
                t, a = tile // 2, tile % 2
                w = min(BAND, P * (t + 1))
                pe.wait_ge(pt_ready, g * (2 * QT) + (tile + 1))
                if tile >= 2:
                    pe.wait_ge(o_free, g * (2 * QT) + (tile - 1))
                for b in range(w // P):
                    for part in (0, 1):
                        last = pe.matmul(O_ps[a], PT[:, a, part, P * b:P * (b + 1)],
                                         VV[:, t + 1 - w // P + b, :],
                                         start=(b == 0 and part == 0), stop=(b == w // P - 1 and part == 1))
                last.then_inc(o_done, 1)

            def turn_values(slot, half):
                for c in range(QT // 2):
                    first = HALF * half + P * c
                    last = pe.transpose(v_ps[slot][half][:, P * c:P * (c + 1)], v_in[:, first:first + P], ident)
                last.then_inc(av_turned, 1)

            def attention(g, slot, n):
                pe.wait_ge(v_half, g + 1)
                turn_values(slot, 0)
                for tile in range(2 * QT):
                    t, a = tile // 2, tile % 2
                    w = min(BAND, P * (t + 1))
                    pe.wait_ge(exp_done, g * (2 * QT) + (tile + 1))
                    if tile >= 2:
                        pe.wait_ge(pt_ready, g * (2 * QT) + (tile - 1))
                    if tile == QT:
                        pe.wait_ge(av_ready, 2 * g + 2)
                    for b in range(w // P):
                        last = pe.transpose(turned[slot][a][:, P * b:P * (b + 1)], prob[a][:, P * b:P * (b + 1)], ident)
                    last.then_inc(pt_done, 1)
                    if tile + 2 < 2 * QT:
                        scores(g, tile + 2)
                    if tile == 0:
                        pe.wait_ge(unit_read, n)
                        turn_values(slot, 1)
                    if tile == 1:
                        pe.wait_ge(av_ready, 2 * g + 1)
                    if tile:
                        attend(g, tile - 1)

            def turn_output(g):
                pe.wait_ge(o_free, g * (2 * QT) + 2 * QT)
                for t in range(QT):
                    last = pe.transpose(PMf[:, P * t:P * (t + 1)], O_sb[:, t, :], ident)
                last.then_inc(ot_done, 1)

            def pair_units(g, j, slot):
                for u in range(3):
                    n = slot + u
                    between = {0: lambda: attend(g - 1, 2 * QT - 1), 1: None, 2: lambda: first_scores(g)}[u]
                    unit(j + n // 2, n % 2, G_hi, G_lo, between=between, tile=(1, None, KT - 2)[u],
                         first_done=v_half_done if u == 2 else None)
                    if u == 0:
                        turn_output(g - 1)

            j = N_ATT // 2
            unit(j, 0, G_hi, G_lo, g_ready, 2 * KT, between=lambda: norm_sums(2), tile=KT - 1)
            unit(j, 1, G_hi, G_lo, between=lambda: spread(2), tile=2)
            unit(j + 1, 0, G_hi, G_lo, between=lambda: first_scores(0), first_done=v_half_done)
            attention(0, 0, N_ATT + 3)
            with pe.Fori(0, ATT_GROUPS // 2 - 1) as i:
                for b in (1, 2):
                    pair_units(2 * i + b, j + 3 * i + 3 * b // 2, 3 * b % 2)
                    attention(2 * i + b, 3 * b % 2, N_ATT + 3 * b + 3 + 6 * i)
            g = ATT_GROUPS - 1
            pair_units(g, j + 3 * g // 2, 3 * g % 2)
            attention(g, 3 * g % 2, N_ATT + 3 * g + 3)
            attend(g, 2 * QT - 1)
            turn_output(g)
            phase(N_OUT1 // 2, A_hi, A_lo, a_ready, KT * (FB + 1))
            mlp(3, N_MLP1, FB + 2)
            norm_sums(4)
            spread(4)

        @block.scalar
        def _(act):
            chain = Chain(act, act_step)

            def split_w(j, s):
                if isinstance(j, int) and 2 * j + s >= N_UNITS:
                    return
                act.wait_ge(raw_landed[s], 16 * j + 16)
                if not (isinstance(j, int) and j == 0):
                    act.wait_ge(unit_done, 2 * j + s - 1)
                act.copy(W_hi[:, s, :, :].rearrange("p k n -> p (k n)"), raw[:, s, :]).then_inc(w_hi, 1)

            def split_g(v, m, ready, count):
                at = C_GAIN + KT * v + m
                act.wait_ge(ready, count)
                act.activation(G_hi[:, m, :], X[:, m, :], ACT.Copy, scale=C[:, at:at + 1]).then_inc(g_hi, 1)

            def square_x(v, m):
                if m >= (2 if v else EARLY + 2):
                    act.wait_ge(ss_added, squares(v, m - 2))
                act.activation(T[:, 2 + m % 2, :], X[:, m, :], ACT.Square).then_inc(sq_ready, 1)

            def norm_root(v):
                act.wait_ge(stat_done, v + 1)
                act.activation(root[:, 0:QT], PM[:, 0, 0:QT], ACT.Sqrt, bias=eps[:, 0:1],
                               scale=P / D).then_inc(sd_ready, 1)

            def norm_scale(v):
                act.wait_ge(spread_done, v + 1)
                act.copy(R[:, :], PMf[:, 0:S]).then_inc(r_ready, 1)

            def split_a(at, src, m):
                act.wait_ge(a_src, at + 1)
                act.copy(A_hi[:, m, :], src).then_inc(a_hi, 1)

            split_w(0, 0)
            act.wait_ge(const_landed, 16)
            act.wait_ge(const_set, 1)
            for m in range(KT):
                split_g(0, m, x_first[m], 16)
                if m == 1:
                    split_w(0, 1)
            for m in range(EARLY, KT):
                square_x(0, m)
            split_w(1, 0)
            norm_root(0)
            norm_scale(0)

            def gn_square(h):
                act.wait_ge(gn_centered, h + 1)
                act.activation(sq_head, OT, ACT.Square).then_inc(gn_sq, 1)

            def gn_root(h):
                act.wait_ge(gn_var, h + 1)
                act.activation(root[:, 2 * QT:3 * QT], PM[:, 2, 0:QT], ACT.Sqrt, bias=eps[:, 1:2]).then_inc(gn_sd, 1)

            def gn_split(h):
                at = head_tile(h)
                act.wait_ge(a_src, at + 1)
                act.copy(A_hi[:, bass.ds(at, 1), :], T[:, 3:4, :]).then_inc(a_hi, 1)

            def copy_v(h):
                act.wait_ge(v_turned, h + 1)
                act.copy(V, PMf[:, 0:S]).then_inc(v_ready, 1)
                if isinstance(h, int) and h == 0:
                    act.wait_ge(kd_landed, 16)
                for c in range(HT):
                    at = HT * h + c
                    scale = key_dec[:, at:at + 1] if isinstance(h, int) else key_dec[:, bass.ds(at, 1)]
                    act.activation(k_tok[:, P * c:P * (c + 1)], PM[:, 2, P * c:P * (c + 1)], ACT.Copy,
                                   scale=scale).then_inc(k_decayed, 1)

            def head_end(h):
                j = head_pair(h)
                act.wait_ge(unit_read, 2 * j + 4)
                act.activation(T[:, 3, :], gate, ACT.Sigmoid).then_inc(gate_sigmoid, 1)
                act.wait_ge(state_done, h + 1)
                act.copy(state, PU[:, 0, 0:P]).then_inc(state_ready, 1)
                for half in (0, 1):
                    act.wait_ge(pv_done, h * N_RET + (4 if half == 0 else N_RET))
                    act.copy(OT[:, HALF * half:HALF * (half + 1)], PM[:, 3, :]).then_inc(o_evac, 1)

            split_w(1, 1)
            split_w(2, 0)
            copy_v(0)
            split_w(2, 1)
            head_end(0)
            j = head_pair(0) + 2
            split_w(j + 1, 0)
            gn_square(0)
            split_w(j + 1, 1)
            gn_root(0)
            gn_split(0)
            split_w(j + 2, 0)
            split_a(1, T[:, 2, :], 1)
            split_a(2, T[:, 2, :], 2)
            split_w(j + 2, 1)
            split_a(3, T[:, 2, :], 3)
            j = head_pair(1)
            split_w(j + 1, 0)
            split_a(4, T[:, 2, :], 4)
            split_w(j + 1, 1)
            split_w(j + 2, 0)
            copy_v(1)
            split_w(j + 2, 1)
            head_end(1)
            with act.Fori(2, RET_HEADS) as h:
                j = head_pair(h)
                split_w(j + 1, 0)
                gn_square(h - 1)
                split_w(j + 1, 1)
                gn_root(h - 1)
                gn_split(h - 1)
                split_w(j + 2, 0)
                copy_v(h)
                split_w(j + 2, 1)
                head_end(h)
            gn_square(RET_HEADS - 1)
            gn_root(RET_HEADS - 1)
            gn_split(RET_HEADS - 1)

            def finish_norm(v, j0):
                for m in range(KT):
                    split_w(j0 + 1 + m // 2, m % 2)
                    if v < 4:
                        split_g(v, m, unit_read, 2 * j0 + m + 1)
                    else:
                        act.wait_ge(unit_read, 2 * j0 + m + 1)
                    square_x(v, m)
                norm_root(v)
                norm_scale(v)

            def mlp_in(n0, fill, fb):
                per = 2
                with act.Fori(0, KT // 2) as i:
                    outer = chain.enter(i, per)
                    for s in (0, 1):
                        act.wait_ge(unit_read, n0 + fb * (2 * KT) + 2 * i + (s + 1))
                        chain.link(act.activation(T[:, 2 + s, :], T[:, s, :], ACT.Square))
                        act.copy(A_hi[:, bass.ds(2 * i + s, 1), :], T[:, 2 + s:3 + s, :]).then_inc(a_hi, 1)
                        split_w(n0 // 2 + fb * KT + i + 1, s)
                    chain.leave(outer, per, KT // 2)

            def mlp(v, n0, fill):
                per = KT
                with act.Fori(0, FB - 1) as fb:
                    outer = chain.enter(fb, per)
                    mlp_in(n0, fill, fb)
                    with act.Fori(0, KT // 2) as i:
                        for s in (0, 1):
                            split_w((n0 + KT) // 2 + fb * KT + i + 1, s)
                    chain.leave(outer, per, FB - 1)
                mlp_in(n0, fill, FB - 1)
                finish_norm(v, (n0 + KT) // 2 + (FB - 1) * KT)

            finish_norm(1, N_OUT0 // 2)
            mlp(2, N_MLP0, 1)

            def exp_tile(g, tile):
                a, w = tile % 2, min(BAND, P * (tile // 2 + 1))
                act.wait_ge(negm_ready, g * (2 * QT) + (tile + 1))
                act.activation(prob[a][:, 0:w], prob[a][:, 0:w], ACT.Exp, scale=-1.0,
                               bias=row[:, tile:tile + 1], accum_out=row[:, 16 + tile:17 + tile]).then_inc(exp_done, 1)

            def values_hi(g, slot, half):
                act.wait_ge(av_turned, 2 * g + half + 1)
                act.copy(VV[:, QT // 2 * half:QT // 2 * (half + 1), 0:P],
                         v_ps[slot][half].rearrange("p (k n) -> p k n", k=QT // 2)).then_inc(av_hi, 1)

            def attention(g, slot):
                values_hi(g, slot, 0)
                for tile in range(2 * QT):
                    a, w = tile % 2, min(BAND, P * (tile // 2 + 1))
                    act.wait_ge(pt_done, g * (2 * QT) + (tile + 1))
                    act.copy(PT[:, a, 0, 0:w], turned[slot][a][:, 0:w]).then_inc(pt_hi, 1)
                    if tile + 2 < 2 * QT:
                        exp_tile(g, tile + 2)
                    if tile == 1:
                        values_hi(g, slot, 1)

            def hi_parts(u, g, n):
                act.wait_ge(unit_read, n)
                src, to = (q_in, Q_s) if u == 0 else (k_in, K_s)
                for a in (0, 1):
                    own = slice(DH * a, DH * (a + 1))
                    act.copy(to[a][own, :], src[own, :]).then_inc(qk_hi, 1)

            def output_hi(g):
                act.wait_ge(ot_done, g + 1)
                act.copy(A_hi[:, bass.ds(g, 1), :] if not isinstance(g, int) else A_hi[:, g, :],
                         PMf[:, 0:S] if isinstance(g, int) else
                         PMf[:, 0:S].rearrange("p (o n) -> p o n", o=1)).then_inc(a_hi, 1)

            def pair(g, j, slot, n):
                hi_parts(0, g, n + 1)
                split_w(j + (slot + 2) // 2, slot)
                if not isinstance(g, int) or g:
                    output_hi(g - 1)
                hi_parts(1, g, n + 2)
                split_w(j + (slot + 3) // 2, 1 - slot)
                exp_tile(g, 0)
                exp_tile(g, 1)
                attention(g, slot)
                split_w(j + (slot + 4) // 2, slot)

            j = N_ATT // 2
            pair(0, j, 0, N_ATT)
            with act.Fori(0, ATT_GROUPS // 2 - 1) as i:
                for b in (1, 2):
                    pair(2 * i + b, j + 3 * i + 3 * b // 2, 3 * b % 2, N_ATT + 3 * b + 6 * i)
            g = ATT_GROUPS - 1
            pair(g, j + 3 * g // 2, 3 * g % 2, N_ATT + 3 * g)
            output_hi(g)
            finish_norm(3, N_OUT1 // 2)
            mlp(4, N_MLP1, FB + 2)

        @block.vector
        def _(dve):
            chain = Chain(dve, dve_step)
            link = chain.link

            def banks(s):
                return PUf[:, S * s:S * (s + 1)]

            def split_w(j, s):
                if isinstance(j, int) and 2 * j + s >= N_UNITS:
                    return
                dve.wait_ge(w_hi, 2 * j + s + 1)
                dve.tensor_tensor(W_lo[:, s, :, :].rearrange("p k n -> p (k n)"), raw[:, s, :],
                                  W_hi[:, s, :, :].rearrange("p k n -> p (k n)").bitcast(F32),
                                  ALU.subtract).then_inc(w_lo, 1)

            def split_g(v, m):
                at = C_GAIN + KT * v + m
                dve.wait_ge(g_hi, KT * v + m + 1)
                dve.scalar_tensor_tensor(out=G_lo[:, m, :], in0=X[:, m, :], scalar=C[:, at:at + 1],
                                         in1=G_hi[:, m, :].bitcast(F32), op0=ALU.mult,
                                         op1=ALU.subtract).then_inc(g_ready, 1)

            def add_squares(v, m):
                dve.wait_ge(sq_ready, squares(v, m))
                buffer = T[:, 2 + m % 2, :]
                if m == 0:
                    dve.tensor_copy(R[:, :], buffer).then_inc(ss_added, 1)
                elif (v, m) == (0, EARLY):
                    dve.wait_ge(early_squares, 2 * EARLY - 1)
                    dve.tensor_tensor(R[:, :], B[0][:, :], buffer, ALU.add).then_inc(ss_added, 1)
                else:
                    dve.wait_ge(ss_added, squares(v, m) - 1)
                    dve.tensor_tensor(R[:, :], R[:, :], buffer, ALU.add).then_inc(ss_added, 1)

            def inverse_root(v):
                dve.wait_ge(sd_ready, v + 1)
                dve.reciprocal(root[:, QT:2 * QT], root[:, 0:QT]).then_inc(inv_ready, 1)
                dve.wait_ge(r_ready, v + 1)

            def done(j, s):
                dve.wait_ge(unit_done, 2 * j + s + 1)

            dve.memset(ones_h[:, :], 1.0 / P)
            dve.memset(row[:, 48:49], 0.0)
            dve.memset(eps[:, 0:1], RMS_EPS)
            dve.memset(eps[:, 1:2], GN_EPS).then_inc(const_set, 1)
            dve.wait_ge(const_landed, 16)
            split_w(0, 0)
            for m in range(KT):
                split_g(0, m)
                if m == 1:
                    split_w(0, 1)
            for m in range(EARLY, KT):
                add_squares(0, m)
            split_w(1, 0)
            inverse_root(0)

            def rotate(j, s, dst, before):
                done(j, s)
                if not (isinstance(before, int) and before == 0):
                    dve.wait_ge(rotated, before)
                dve.tensor_tensor(dst, banks(s), cosR, ALU.mult)
                dve.tensor_tensor(T[0:64, 2, :], banks(s)[64:128], sinR[0:64], ALU.mult)
                ins = dve.tensor_tensor(T[64:128, 2, :], banks(s)[0:64], sinR[64:128], ALU.mult)
                ins.then_inc(unit_read, 1)
                dve.wait_ge(unit_read, 2 * j + s + 1)
                dve.tensor_tensor(dst, dst, T[:, 2, :], ALU.add).then_inc(rotated, 1)

            def gn_center(h):
                dve.wait_ge(gn_mean, h + 1)
                dve.tensor_tensor(OT, OT, PMf[:, 0:S], ALU.subtract).then_inc(gn_centered, 1)

            def gn_scale(h):
                dve.wait_ge(gn_sd, h + 1)
                dve.reciprocal(root[:, 3 * QT:4 * QT], root[:, 2 * QT:3 * QT]).then_inc(gn_inv, 1)
                dve.wait_ge(gn_spread, h + 1)
                link(dve.tensor_tensor(T[:, 3, :], PMf[:, S:2 * S], OT, ALU.mult))
                gain = C[:, C_GN + h:C_GN + h + 1] if isinstance(h, int) else C[:, bass.ds(h + C_GN, 1)]
                dve.scalar_tensor_tensor(out=T[:, 3, :], in0=T[:, 3, :], scalar=gain, in1=gate, op0=ALU.mult,
                                         op1=ALU.mult).then_inc(a_src, 1)
                at = head_tile(h)
                dve.wait_ge(a_hi, at + 1)
                dve.tensor_tensor(A_lo[:, bass.ds(at, 1), :], T[:, 3:4, :], A_hi[:, bass.ds(at, 1), :].bitcast(F32),
                                  ALU.subtract).then_inc(a_ready, 1)

            def head(h, norm=True):
                j = head_pair(h)
                after_pooling = isinstance(h, int) and h == 1
                if after_pooling:
                    dve.wait_ge(a_ready, POOL_GROUPS)
                rotate(j, 0, qT, 2 * h)
                split_w(j + 1, 0)
                if norm:
                    gn_center(h - 1)
                if after_pooling:
                    dve.wait_ge(rotated, 2 * h + 1)
                    pool_scale(3)
                    dve.wait_ge(a_ready, POOL_GROUPS + 1)
                rotate(j, 1, kT, 2 * h + 1)
                split_w(j + 1, 1)
                if norm:
                    gn_scale(h - 1)
                done(j + 1, 0)
                dve.tensor_tensor(vT, banks(0), R[:, :], ALU.mult).then_inc(unit_read, 1)
                split_w(j + 2, 0)
                head_end(h)

            def head_end(h):
                j = head_pair(h)
                done(j + 1, 1)
                dve.tensor_tensor(gate, banks(1), R[:, :], ALU.mult).then_inc(unit_read, 1)
                split_w(j + 2, 1)
                dve.wait_ge(dec_landed, 16 * h + 16)
                for x, (q0, n, kt) in enumerate(RET_STEPS):
                    dve.wait_ge(score_done, h * N_RET + (x + 1))
                    if x == 3:
                        dve.tensor_tensor(q_late, qT[:, HALF:S], dec[:, HALF:S], ALU.mult).then_inc(q_decayed, 1)
                    if x >= 3:
                        dve.wait_ge(pv_done, h * N_RET + (x - 2))
                    dve.tensor_tensor(probs[x % 3][:, 0:n], PM[:, x % 3, 0:n],
                                      dec[:, q0 - P * kt:q0 - P * kt + n], ALU.mult).then_inc(p_ready, 1)
                dve.wait_ge(gate_sigmoid, h + 1)
                dve.tensor_tensor(gate, gate, T[:, 3, :], ALU.mult)

            def pool_window(j, s, i):
                done(j, s)
                if i:
                    dve.wait_ge(pooled, i)
                tok = X[:, 0, :]
                ins = dve.tensor_tensor(tok, banks(s), R[:, :], ALU.mult)
                ins.then_inc(unit_read, 1)
                dve.wait_ge(unit_read, 2 * j + s + 1)
                cur = tok
                for step in range(i + 1):
                    lag = 1 << step
                    nxt = X[:, 1 if step % 2 == 0 else 3, :]
                    dve.tensor_copy(nxt[:, 0:lag], cur[:, 0:lag])
                    link(dve.tensor_tensor(nxt[:, lag:S], cur[:, lag:S], cur[:, 0:S - lag], ALU.add))
                    cur = nxt
                y = X[:, 6 + i % 2, :]
                if i >= 2:
                    dve.wait_ge(pool_mm, i - 1)
                cnt = C[:, C_CNT + EDGE * i:C_CNT + EDGE * (i + 1)]
                link(dve.tensor_tensor(y[:, 0:EDGE], cur[:, 0:EDGE], cnt, ALU.mult))
                dve.tensor_tensor(y[:, 0:EDGE], y[:, 0:EDGE], tok[:, 0:EDGE], ALU.subtract)
                dve.scalar_tensor_tensor(out=y[:, EDGE:S], in0=cur[:, EDGE:S], scalar=1.0 / POOL_WINDOWS[i],
                                         in1=tok[:, EDGE:S], op0=ALU.mult, op1=ALU.subtract).then_inc(pooled, 1)

            def pool_scale(i):
                dve.wait_ge(pool_mm, i + 1)
                dve.wait_ge(a_ready, i + 1)
                dve.tensor_scalar(T[:, 2, :], PMf[:, S * (i % 2):S * (i % 2 + 1)], C[:, C_PS + i:C_PS + i + 1],
                                  None, ALU.mult).then_inc(a_src, 1)
                dve.wait_ge(a_hi, i + 2)
                dve.tensor_tensor(A_lo[:, i + 1, :], T[:, 2, :], A_hi[:, i + 1, :].bitcast(F32),
                                  ALU.subtract).then_inc(a_ready, 1)

            done(0, 0)
            dve.tensor_tensor(vT, banks(0), R[:, :], ALU.mult).then_inc(unit_read, 1)
            dve.wait_ge(rot_landed, 16)
            link(dve.tensor_tensor(cosR, cosR, R[:, :], ALU.mult))
            link(dve.tensor_tensor(sinR, sinR, R[:, :], ALU.mult))
            rotate(0, 1, qT, 0)
            split_w(1, 1)
            rotate(1, 0, kT, 1)
            split_w(2, 0)
            head_end(0)
            j = head_pair(0) + 2
            pool_window(j, 0, 0)
            split_w(j + 1, 0)
            gn_center(0)
            pool_window(j, 1, 1)
            split_w(j + 1, 1)
            gn_scale(0)
            pool_window(j + 1, 0, 2)
            split_w(j + 2, 0)
            pool_scale(0)
            pool_scale(1)
            pool_window(j + 1, 1, 3)
            split_w(j + 2, 1)
            pool_scale(2)
            head(1, norm=False)
            with dve.Fori(2, RET_HEADS) as h:
                outer = chain.enter(h - 2, 1)
                head(h)
                chain.leave(outer, 1, RET_HEADS - 2)
            gn_center(RET_HEADS - 1)
            gn_scale(RET_HEADS - 1)

            def add_unit(j, s, m):
                done(j, s)
                x = X[:, m, :] if isinstance(m, int) else X[:, bass.ds(m, 1), :]
                src = banks(s) if isinstance(m, int) else banks(s).rearrange("p (o n) -> p o n", o=1)
                return dve.tensor_tensor(x, x, src, ALU.add)

            def finish_norm(v, j0, landed=0):
                for m in range(KT):
                    if landed:
                        dve.wait_ge(x_landed[m], landed)
                    add_unit(j0 + m // 2, m % 2, m).then_inc(unit_read, 1)
                    dve.wait_ge(unit_read, 2 * j0 + m + 1)
                    if v < 4:
                        split_g(v, m)
                    split_w(j0 + 1 + m // 2, m % 2)
                    add_squares(v, m)
                inverse_root(v)

            def mlp_in(n0, fill, fb):
                with dve.Fori(0, KT // 2) as i:
                    for s in (0, 1):
                        j = n0 // 2 + fb * KT + i
                        at = KT * fill + fb * KT + 2 * i + s
                        done(j, s)
                        dve.scalar_tensor_tensor(out=T[:, s, :], in0=banks(s), scalar=0.0, in1=R[:, :], op0=ALU.max,
                                                 op1=ALU.mult).then_inc(unit_read, 1)
                        dve.wait_ge(a_hi, at + 1)
                        dve.tensor_tensor(A_lo[:, bass.ds(2 * i + s, 1), :], T[:, 2 + s:3 + s, :],
                                          A_hi[:, bass.ds(2 * i + s, 1), :].bitcast(F32),
                                          ALU.subtract).then_inc(a_ready, 1)
                        split_w(j + 1, s)

            def mlp(v, n0, fill):
                with dve.Fori(0, FB - 1) as fb:
                    mlp_in(n0, fill, fb)
                    with dve.Fori(0, KT // 2) as i:
                        for s in (0, 1):
                            j = (n0 + KT) // 2 + fb * KT + i
                            add_unit(j, s, 2 * i + s).then_inc(unit_read, 1)
                            split_w(j + 1, s)
                mlp_in(n0, fill, FB - 1)
                finish_norm(v, (n0 + KT) // 2 + (FB - 1) * KT)

            finish_norm(1, N_OUT0 // 2, landed=16)
            mlp(2, N_MLP0, 1)
            dve.wait_ge(spilled, 16 * KT)

            def output(g, tile, part):
                t, a = tile // 2, tile % 2
                to, share = O_sb[:, t, DH * a:DH * (a + 1)], row[:, 32 + tile:33 + tile]
                of = O_ps[a][:, P * part + DH * a:P * part + DH * (a + 1)]
                if part == 0:
                    dve.wait_ge(share_ready, g * (2 * QT) + (tile + 1))
                    dve.wait_ge(o_done, g * (2 * QT) + (tile + 1))
                    link(dve.tensor_scalar(to, of, share, None, ALU.mult))
                else:
                    dve.scalar_tensor_tensor(out=to, in0=of, scalar=share, in1=to, op0=ALU.mult,
                                             op1=ALU.add).then_inc(o_free, 1)

            def biased(g, tile):
                a, w = tile % 2, min(BAND, P * (tile // 2 + 1))
                banks = 2 if w > HALF else 1
                first = tile % 2 if banks == 1 else 0
                dve.wait_ge(s_done, g * (2 * QT) + (tile + 1))
                dve.memset(row[:, 32 + tile:33 + tile], 0.0)
                two = [x.rearrange("p (c n) -> p c n", c=banks) for x in (prob[a][:, 0:w], bias[a][:, BAND - w:BAND])]
                dve.tensor_tensor_reduce(two[0], PM[:, first:first + banks, 0:w // banks], two[1], -1.0,
                                         3.0e38, ALU.add, ALU.min, row[:, tile:tile + 1]).then_inc(negm_ready, 1)

            def values_lo(g, slot, half):
                tokens = slice(QT // 2 * half, QT // 2 * (half + 1))
                dve.wait_ge(av_hi, 2 * g + half + 1)
                dve.tensor_tensor(VV[:, tokens, P:2 * P], v_ps[slot][half].rearrange("p (k n) -> p k n", k=QT // 2),
                                  VV[:, tokens, 0:P].bitcast(F32), ALU.subtract).then_inc(av_ready, 1)

            def attention(g, slot):
                values_lo(g, slot, 0)
                for tile in range(2 * QT):
                    a, w = tile % 2, min(BAND, P * (tile // 2 + 1))
                    if tile + 2 < 2 * QT:
                        biased(g, tile + 2)
                    dve.wait_ge(pt_hi, g * (2 * QT) + (tile + 1))
                    dve.reciprocal(row[:, 32 + tile:33 + tile], row[:, 16 + tile:17 + tile]).then_inc(share_ready, 1)
                    dve.tensor_tensor(PT[:, a, 1, 0:w], turned[slot][a][:, 0:w], PT[:, a, 0, 0:w].bitcast(F32),
                                      ALU.subtract).then_inc(pt_ready, 1)
                    if tile:
                        output(g, tile - 1, 0)
                        output(g, tile - 1, 1)
                    if tile == 1:
                        values_lo(g, slot, 1)
                output(g, 2 * QT - 1, 0)
                output(g, 2 * QT - 1, 1)

            def output_lo(g):
                dve.wait_ge(a_hi, KT * (FB + 1) + g + 1)
                dve.tensor_tensor(A_lo[:, bass.ds(g, 1), :], PMf[:, 0:S].rearrange("p (o n) -> p o n", o=1),
                                  A_hi[:, bass.ds(g, 1), :].bitcast(F32), ALU.subtract).then_inc(a_ready, 1)

            def pair(g, j, slot):
                def at(u):
                    return j + (slot + u) // 2, (slot + u) % 2

                done(*at(0))
                dve.scalar_tensor_tensor(out=q_in, in0=banks(at(0)[1]), scalar=DH ** -0.5, in1=R[:, :],
                                         op0=ALU.mult, op1=ALU.mult).then_inc(unit_read, 1)
                dve.wait_ge(qk_hi, 4 * g + 2)
                for a in (0, 1):
                    own, other = slice(DH * a, DH * (a + 1)), slice(DH * (1 - a), DH * (2 - a))
                    ins = dve.tensor_tensor(Q_s[a][other, :], q_in[own, :], Q_s[a][own, :].bitcast(F32), ALU.subtract)
                ins.then_inc(qk_ready, 1)
                split_w(j + (slot + 2) // 2, slot)
                if not isinstance(g, int) or g:
                    output_lo(g - 1)
                done(*at(1))
                dve.tensor_tensor(k_in, banks(at(1)[1]), R[:, :], ALU.mult).then_inc(unit_read, 1)
                dve.wait_ge(unit_read, 2 * at(1)[0] + (at(1)[1] + 1))
                for a in (0, 1):
                    own, other = slice(DH * a, DH * (a + 1)), slice(DH * (1 - a), DH * (2 - a))
                    dve.tensor_copy(K_s[a][other, :], k_in[own, :])
                dve.wait_ge(qk_hi, 4 * g + 4)
                for a in (0, 1):
                    own = slice(DH * a, DH * (a + 1))
                    ins = dve.tensor_tensor(K_lo[own, :], k_in[own, :], K_s[a][own, :].bitcast(F32), ALU.subtract)
                ins.then_inc(qk_ready, 1)
                split_w(j + (slot + 3) // 2, 1 - slot)
                if isinstance(g, int) and g == 0:
                    dve.wait_ge(b_masked, 4)
                dve.wait_ge(b_ready, g * 8 + 8)
                biased(g, 0)
                biased(g, 1)
                for half, read in ((0, v_half), (1, unit_read)):
                    if half == 0:
                        dve.wait_ge(v_half_done, g + 1)
                    else:
                        done(*at(2))
                    part = slice(HALF * half, HALF * (half + 1))
                    dve.tensor_tensor(v_in[:, part], banks(at(2)[1])[:, part], R[:, part], ALU.mult).then_inc(read, 1)
                attention(g, slot)
                split_w(j + (slot + 4) // 2, slot)

            j = N_ATT // 2
            per = 2 * QT
            pair(0, j, 0)
            with dve.Fori(0, ATT_GROUPS // 2 - 1) as i:
                outer = chain.enter(i, 2 * per)
                for b in (1, 2):
                    pair(2 * i + b, j + 3 * i + 3 * b // 2, 3 * b % 2)
                chain.leave(outer, 2 * per, ATT_GROUPS // 2 - 1)
            g = ATT_GROUPS - 1
            pair(g, j + 3 * g // 2, 3 * g % 2)
            output_lo(g)
            finish_norm(3, N_OUT1 // 2, landed=32)
            mlp(4, N_MLP1, FB + 2)
            for m in range(KT):
                at = C_GAIN + KT * 4 + m
                dve.scalar_tensor_tensor(out=X[:, m, :], in0=X[:, m, :], scalar=C[:, at:at + 1], in1=R[:, :],
                                         op0=ALU.mult, op1=ALU.mult).then_inc(y_ready, 1)


def _units(w):
    rows, cols = w.shape[0] // D, w.shape[1] // P
    return w.reshape(rows, KT, P, cols, P).transpose(0, 3, 2, 1, 4).reshape(rows * cols, P, D)


def _tables():
    import numpy as np
    f = np.float32
    half = P // 2
    inv_freq = f(1.0) / np.power(f(10000.0), np.linspace(0.0, 1.0, half, dtype=f), dtype=f)
    ang = (np.arange(S, dtype=f)[:, None] * inv_freq[None, :]).astype(f).T
    cos, sin = np.cos(ang.astype(np.float64)), np.sin(ang.astype(np.float64))
    rot = np.stack([np.concatenate([cos, cos]), np.concatenate([-sin, sin])], 1).astype(f)
    p, c = np.arange(P)[:, None], np.arange(HALF)[None, :]
    log_g = np.log1p(-np.exp2(-5.0 - np.arange(RET_HEADS)))
    decay = np.exp(np.abs(c - p)[None] * log_g[:, None, None])
    decay = np.where(c // DH < p // DH, 0.0, decay) * P ** -0.5
    from_half = np.exp(np.broadcast_to(c, (P, HALF))[None] * log_g[:, None, None])
    decay = np.concatenate([decay, from_half], axis=2)
    t = np.arange(HT)[None, None, :]
    key_decay = np.exp((HALF - P * t - p[:, :, None]) * log_g[None, :, None]) * P ** -0.5
    tokens = np.arange(EDGE) + 1
    cnt = np.concatenate([1.0 / np.minimum(tokens, w) for w in POOL_WINDOWS])
    return rot, decay.astype(f), key_decay.reshape(P, RET_HEADS * HT).astype(f), cnt.astype(f)


def kernel(x, mix_norm, ffn_norm, w_ffn_in, w_ffn_out, ab_w_in, ab_gn_gain, ab_w_pool, ab_pool_scale, ab_w_out,
           c_w_qkv, c_rel_bias, c_w_out, final_norm):
    import numpy as np
    import concourse.bacc as bacc
    from concourse.bass_utils import run_bass_kernel_spmd

    (x, mix_norm, ffn_norm, w_ffn_in, w_ffn_out, ab_w_in, ab_gn_gain, ab_w_pool, ab_pool_scale, ab_w_out, c_w_qkv,
     c_rel_bias, c_w_out, final_norm) = map(np.asarray, (
         x, mix_norm, ffn_norm, w_ffn_in, w_ffn_out, ab_w_in, ab_gn_gain, ab_w_pool, ab_pool_scale, ab_w_out, c_w_qkv,
         c_rel_bias, c_w_out, final_norm))

    ret = RET_HEADS * P
    w_in = ab_w_in[0]
    turned = np.concatenate([np.arange(0, P, 2), np.arange(1, P, 2)])
    parts = []
    for h in range(RET_HEADS):
        for part in (2, 0, 1, 3) if h == 0 else range(4):
            w = w_in[:, part * ret + h * P:part * ret + (h + 1) * P]
            parts.append(_units(w[:, turned] if part < 2 else w))
        if h == 0:
            parts.append(_units(w_in[:, 4 * ret:]))
    made = [0, *range(RET_HEADS, RET_HEADS + POOL_GROUPS), *range(1, RET_HEADS)]
    parts.append(_units(ab_w_out[0].reshape(KT, P, D)[made].reshape(D, D)))

    def mlp(layer):
        for fb in range(FB):
            parts.append(_units(w_ffn_in[layer][:, fb * D:(fb + 1) * D]))
            parts.append(_units(w_ffn_out[layer][fb * D:(fb + 1) * D]))

    mlp(0)
    for g in range(ATT_GROUPS):
        parts.extend(_units(c_w_qkv[0][:, part * D + g * P:part * D + (g + 1) * P]) for part in range(3))
    parts.append(_units(c_w_out[0]))
    mlp(1)
    weights = np.concatenate(parts)

    rot, decay, key_decay, cnt = _tables()
    norms = [mix_norm[0], ffn_norm[0], mix_norm[1], ffn_norm[1], final_norm]
    small = np.concatenate(
        [np.eye(P, dtype=np.float32)] + [g.reshape(KT, P).T for g in norms]
        + [ab_gn_gain[0].reshape(RET_HEADS, P).T, ab_pool_scale[0].reshape(POOL_GROUPS, P).T,
           np.broadcast_to(cnt, (P, cnt.size))], axis=1)
    n_rel = c_rel_bias.shape[-1]
    rel = c_rel_bias[0][:, np.minimum(1 + np.arange(REL_ROW), n_rel - 1)]
    arrays = {
        "weights": weights,
        "x_in": x[0].T.reshape(KT, P, S),
        "small": small,
        "rot": rot,
        "decay": decay,
        "key_decay": key_decay,
        "w_pool": ab_w_pool[0].transpose(1, 0, 2).reshape(P, POOL_GROUPS * P),
        "rel": rel,
    }
    arrays = {name: np.ascontiguousarray(a) for name, a in arrays.items()}
    nc = bacc.Bacc("TRN2", target_bir_lowering=False, num_devices=1)
    args = [nc.dram_tensor(name, a.shape, F32, kind="ExternalInput").ap() for name, a in arrays.items()]
    out = nc.dram_tensor("out", (KT, P, S), F32, kind="ExternalOutput").ap()
    spill = nc.dram_tensor("spill", (KT, P, S), F32).ap()
    trunk_kernel(nc, *args, out, spill)
    result = run_bass_kernel_spmd(nc, [arrays], core_ids=[0]).results[0]["out"]
    return np.ascontiguousarray(result.reshape(D, S).T)[None]
```
